# Optimizing a Trainium2 kernel written in Bass

```python
import math
import jax, jax.numpy as jnp
from jax import lax
import numpy as np

D_MODEL = 1024
BATCH = 1
SEQ = 512
DEPTH = 1
DEC_BATCH = 1
DEC_SEQ = 512
PAST_LEN = 128

GRID_W = 64
EPS = 1e-6
SSD_HEAD_DIM = 64
D_INNER = D_MODEL // 2
SSD_HEADS = D_INNER // SSD_HEAD_DIM
SSD_GROUPS = 2
SSD_STATE = 64
SSD_CHUNK = 128
CONV_W = 4
CONV_LEFT = (CONV_W - 1) // 2
CONV_CH = D_INNER + 2 * SSD_GROUPS * SSD_STATE
DT_MIN = 0.001
DT_MAX = 0.1
NA_HEADS = 4
NA_HEAD_DIM = D_MODEL // 16
NA_WIDTH = NA_HEADS * NA_HEAD_DIM
NA_MAX_KH = 8
NA_KW = 16
POOL_WINDOWS = (2, 4, 8, 16)
POOL_GROUPS = 4
POOL_WIDTH = D_MODEL - D_INNER - NA_WIDTH
POOL_GROUP_DIM = POOL_WIDTH // POOL_GROUPS
D_MIX = D_INNER + NA_WIDTH + POOL_WIDTH
D_IN = D_INNER + CONV_CH + 2 * SSD_HEADS + 3 * NA_WIDTH + POOL_WIDTH
SPLIT_POINTS = (D_INNER, D_INNER + CONV_CH, D_INNER + CONV_CH + 2 * SSD_HEADS, D_INNER + CONV_CH + 2 * SSD_HEADS + NA_WIDTH, D_INNER + CONV_CH + 2 * SSD_HEADS + 2 * NA_WIDTH, D_INNER + CONV_CH + 2 * SSD_HEADS + 3 * NA_WIDTH)
N_MEM = 256
XA_HEADS = 4
XA_HEAD_DIM = D_MODEL // 8
XA_WIDTH = XA_HEADS * XA_HEAD_DIM
N_EXPERT_GROUPS = 4
EXPERTS_PER_GROUP = 8
N_EXPERTS = N_EXPERT_GROUPS * EXPERTS_PER_GROUP
TOP_K = 2
D_EXPERT = D_MODEL // 4
MOE_BLOCK = 128

kernel_name = 'hybrid_ssd_natten_pool_hmoe_encoder'

def rms_norm(x, g):
    xf = x.astype(jnp.float32)
    y = xf * lax.rsqrt(jnp.mean(xf * xf, axis=-1, keepdims=True) + EPS)
    return (y * g.astype(jnp.float32)).astype(x.dtype)

def centred_depthwise_conv(u, w, b):
    T = u.shape[1]
    up = jnp.pad(u, ((0, 0), (CONV_LEFT, CONV_W - 1 - CONV_LEFT), (0, 0)))
    out = b
    for j in range(CONV_W):
        out = out + up[:, j:j + T] * w[j]
    return out

def ssd_chunked_scan(xh, dt, a, bm, cm):
    b, T, H, P = xh.shape
    G, N = bm.shape[2], bm.shape[3]
    R = H // G
    L = SSD_CHUNK
    nc = T // L
    la = (dt * a).reshape(b, nc, L, G, R)
    xdt = (xh.astype(jnp.float32) * dt[..., None]).reshape(b, nc, L, G, R, P)
    bc = bm.astype(jnp.float32).reshape(b, nc, L, G, N)
    cc = cm.astype(jnp.float32).reshape(b, nc, L, G, N)
    cs = jnp.cumsum(la, axis=2)
    tri = jnp.tril(jnp.ones((L, L), dtype=bool))
    seg = cs[:, :, :, None] - cs[:, :, None, :]
    decay = jnp.exp(jnp.where(tri[None, None, :, :, None, None], seg, -jnp.inf))
    cb = jnp.einsum('bclgn,bcsgn->bclsg', cc, bc)
    y_diag = jnp.einsum('bclsg,bclsgr,bcsgrp->bclgrp', cb, decay, xdt)
    decay_end = jnp.exp(cs[:, :, -1:] - cs)
    states = jnp.einsum('bclgn,bclgr,bclgrp->bcgrpn', bc, decay_end, xdt)
    chunk_decay = jnp.exp(cs[:, :, -1])

    def step(s, inp):
        st, dec = inp
        return s * dec[..., None, None] + st, s

    init = jnp.zeros((b, G, R, P, N), jnp.float32)
    _, s_in = lax.scan(step, init, (jnp.moveaxis(states, 1, 0), jnp.moveaxis(chunk_decay, 1, 0)))
    s_in = jnp.moveaxis(s_in, 0, 1)
    y_off = jnp.einsum('bclgn,bcgrpn,bclgr->bclgrp', cc, s_in, jnp.exp(cs))
    return (y_diag + y_off).reshape(b, T, H, P)

def ssd_heads(z, xbc_raw, dt_raw, conv_w, conv_b, dt_bias, a_log, d_skip, ssd_norm):
    b, T, _ = z.shape
    gn = SSD_GROUPS * SSD_STATE
    xbc = jax.nn.silu(centred_depthwise_conv(xbc_raw, conv_w, conv_b))
    xs = xbc[..., :D_INNER].reshape(b, T, SSD_HEADS, SSD_HEAD_DIM)
    bm = xbc[..., D_INNER:D_INNER + gn].reshape(b, T, SSD_GROUPS, SSD_STATE)
    cm = xbc[..., D_INNER + gn:].reshape(b, T, SSD_GROUPS, SSD_STATE)
    dtf = dt_raw.astype(jnp.float32)
    dt_fwd = jax.nn.softplus(dtf[..., :SSD_HEADS] + dt_bias[0].astype(jnp.float32))
    dt_bwd = jax.nn.softplus(dtf[..., SSD_HEADS:] + dt_bias[1].astype(jnp.float32))
    a_fwd = -jnp.exp(a_log[0].astype(jnp.float32))
    a_bwd = -jnp.exp(a_log[1].astype(jnp.float32))
    rev = lambda u: jnp.flip(u, axis=1)
    y_f = ssd_chunked_scan(xs, dt_fwd, a_fwd, bm, cm)
    y_b = rev(ssd_chunked_scan(rev(xs), rev(dt_bwd), a_bwd, rev(bm), rev(cm)))
    y = y_f + y_b + d_skip.astype(jnp.float32)[:, None] * xs.astype(jnp.float32)
    y = y.reshape(b, T, D_INNER) * jax.nn.silu(z.astype(jnp.float32))
    y = y.reshape(b, T, SSD_GROUPS, D_INNER // SSD_GROUPS)
    y = y * lax.rsqrt(jnp.mean(y * y, axis=-1, keepdims=True) + EPS)
    return (y.reshape(b, T, D_INNER) * ssd_norm.astype(jnp.float32)).astype(z.dtype)

def neighbourhood_attention(q, k, v, q_norm, k_norm, rpb):
    b, T, _ = q.shape
    R = T // GRID_W
    KH = min(NA_MAX_KH, R)
    heads = lambda u: u.reshape(b, R, GRID_W, NA_HEADS, NA_HEAD_DIM)
    qh = rms_norm(heads(q), q_norm)
    kh = rms_norm(heads(k), k_norm)
    vh = heads(v)
    rows = jnp.arange(R)
    row_start = jnp.clip(rows - NA_MAX_KH // 2, 0, R - KH)
    row_idx = row_start[:, None] + jnp.arange(KH)[None, :]
    k_g = kh[:, row_idx]
    v_g = vh[:, row_idx]
    s = jnp.einsum('brqhd,brikhd->bhrqik', qh, k_g).astype(jnp.float32) * (NA_HEAD_DIM ** -0.5)
    cols = jnp.arange(GRID_W)
    col_start = jnp.clip(cols - NA_KW // 2, 0, GRID_W - NA_KW)
    col_mask = (cols[None, :] >= col_start[:, None]) & (cols[None, :] < col_start[:, None] + NA_KW)
    dr = row_idx - rows[:, None] + (NA_MAX_KH - 1)
    dc = jnp.clip(cols[None, :] - cols[:, None] + (NA_KW - 1), 0, 2 * NA_KW - 2)
    bias = rpb.astype(jnp.float32)[:, dr[:, None, :, None], dc[None, :, None, :]]
    s = jnp.where(col_mask[:, None, :], s + bias[None], -jnp.inf)
    p = jax.nn.softmax(s, axis=(-2, -1))
    o = jnp.einsum('bhrqik,brikhd->brqhd', p.astype(v.dtype), v_g)
    return o.reshape(b, T, NA_WIDTH)

def multiscale_pool(u, pool_w, pool_scale):
    b, T, _ = u.shape
    uf = u.astype(jnp.float32).reshape(b, T, POOL_GROUPS, POOL_GROUP_DIM)
    csum = jnp.concatenate([jnp.zeros((b, 1, POOL_GROUPS, POOL_GROUP_DIM), jnp.float32), jnp.cumsum(uf, axis=1)], axis=1)
    t = jnp.arange(T)
    outs = []
    for gi, w in enumerate(POOL_WINDOWS):
        lo = jnp.clip(t - w // 2, 0, T)
        hi = jnp.clip(t + w // 2, 0, T)
        win_sum = csum[:, hi, gi] - csum[:, lo, gi]
        outs.append(win_sum / (hi - lo).astype(jnp.float32)[None, :, None] - uf[:, :, gi])
    d = jnp.stack(outs, axis=2)
    y = jnp.einsum('btgc,gcd->btgd', d, pool_w.astype(jnp.float32)).reshape(b, T, POOL_WIDTH)
    return (y * pool_scale.astype(jnp.float32)).astype(u.dtype)

def memory_cross_attention(hn, memn, w_xq, w_xkv, xq_norm, xk_norm, w_xo):
    b, T, _ = hn.shape
    M = memn.shape[1]
    q = rms_norm((hn @ w_xq).reshape(b, T, XA_HEADS, XA_HEAD_DIM), xq_norm)
    kv = (memn @ w_xkv).reshape(b, M, 2, XA_HEADS, XA_HEAD_DIM)
    k = rms_norm(kv[:, :, 0], xk_norm)
    v = kv[:, :, 1]
    s = jnp.einsum('bthd,bmhd->bhtm', q, k).astype(jnp.float32) * (XA_HEAD_DIM ** -0.5)
    p = jax.nn.softmax(s, axis=-1)
    o = jnp.einsum('bhtm,bmhd->bthd', p.astype(v.dtype), v).reshape(b, T, XA_WIDTH)
    return o @ w_xo

def hier_moe(hn, w_router_group, b_router_group, w_router_expert, b_router_expert, w_e_gate, w_e_up, w_e_down):
    b, T, D = hn.shape
    N = b * T
    A = N * TOP_K
    xt = hn.reshape(N, D)
    g_logits = (xt @ w_router_group).astype(jnp.float32) + b_router_group.astype(jnp.float32)
    g_sel = jnp.argmax(g_logits, axis=-1)
    g_gate = jnp.max(jax.nn.softmax(g_logits, axis=-1), axis=-1, keepdims=True)
    e_logits = ((xt @ w_router_expert).astype(jnp.float32) + b_router_expert.astype(jnp.float32)).reshape(N, N_EXPERT_GROUPS, EXPERTS_PER_GROUP)
    e_in = e_logits[jnp.arange(N), g_sel]
    top_val, top_loc = lax.top_k(e_in, TOP_K)
    gates = jax.nn.softmax(top_val, axis=-1) * g_gate
    e_id = (g_sel[:, None] * EXPERTS_PER_GROUP + top_loc).astype(jnp.int32)
    flat_e = e_id.reshape(A)
    flat_tok = jnp.repeat(jnp.arange(N, dtype=jnp.int32), TOP_K)
    flat_w = gates.reshape(A)
    order = jnp.argsort(flat_e)
    se, stok, sw = flat_e[order], flat_tok[order], flat_w[order]
    sizes = jnp.bincount(flat_e, length=N_EXPERTS)
    start = jnp.cumsum(sizes) - sizes
    psizes = (sizes + MOE_BLOCK - 1) // MOE_BLOCK * MOE_BLOCK
    pend = jnp.cumsum(psizes)
    pstart = pend - psizes
    dest = pstart[se] + (jnp.arange(A) - start[se])
    nb = (A + N_EXPERTS * (MOE_BLOCK - 1) + MOE_BLOCK - 1) // MOE_BLOCK
    P = nb * MOE_BLOCK
    tok_buf = jnp.full((P,), N, jnp.int32).at[dest].set(stok)
    w_buf = jnp.zeros((P,), jnp.float32).at[dest].set(sw)
    blk_expert = jnp.clip(jnp.searchsorted(pend, jnp.arange(nb) * MOE_BLOCK, side='right'), 0, N_EXPERTS - 1)
    x_pad = jnp.concatenate([xt, jnp.zeros((1, D), xt.dtype)], axis=0)

    def expert_block(args):
        idx, wts, e = args
        xb = x_pad[idx]
        hb = jax.nn.silu(xb @ w_e_gate[e]) * (xb @ w_e_up[e])
        return (hb @ w_e_down[e]).astype(jnp.float32) * wts[:, None]

    yb = lax.map(expert_block, (tok_buf.reshape(nb, MOE_BLOCK), w_buf.reshape(nb, MOE_BLOCK), blk_expert))
    out = jnp.zeros((N + 1, D), jnp.float32).at[tok_buf].add(yb.reshape(P, D))[:N]
    return out.reshape(b, T, D).astype(hn.dtype)

def encoder_layer(x, mem, norm_mix, w_in, conv_w, conv_b, dt_bias, a_log, d_skip, ssd_norm, na_q_norm, na_k_norm, na_rpb, pool_w, pool_scale, w_out, norm_xa, norm_mem, w_xq, w_xkv, xq_norm, xk_norm, w_xo, norm_ffn, w_router_group, b_router_group, w_router_expert, b_router_expert, w_e_gate, w_e_up, w_e_down):
    h = rms_norm(x, norm_mix)
    proj = h @ w_in
    z, xbc, dt_raw, q, k, v, u = jnp.split(proj, SPLIT_POINTS, axis=-1)
    y_ssd = ssd_heads(z, xbc, dt_raw, conv_w, conv_b, dt_bias, a_log, d_skip, ssd_norm)
    y_na = neighbourhood_attention(q, k, v, na_q_norm, na_k_norm, na_rpb)
    y_pool = multiscale_pool(u, pool_w, pool_scale)
    mix = jnp.concatenate([y_ssd, y_na.astype(x.dtype), y_pool], axis=-1) @ w_out
    x = x + mix.astype(x.dtype)
    x = x + memory_cross_attention(rms_norm(x, norm_xa), rms_norm(mem, norm_mem), w_xq, w_xkv, xq_norm, xk_norm, w_xo).astype(x.dtype)
    x = x + hier_moe(rms_norm(x, norm_ffn), w_router_group, b_router_group, w_router_expert, b_router_expert, w_e_gate, w_e_up, w_e_down)
    return x

def setup_inputs(seed: int = 0) -> dict:
    key = jax.random.key(seed)
    ks = jax.random.split(key, 40)
    f32 = jnp.float32

    def nrm(k, shape, scale):
        return jax.random.normal(k, shape, f32) * scale

    def gain(k, shape):
        return 1.0 + nrm(k, shape, 0.02)

    dt0 = jnp.exp(jax.random.uniform(ks[8], (DEPTH, 2, SSD_HEADS), f32, math.log(DT_MIN), math.log(DT_MAX)))
    dt_bias = dt0 + jnp.log(-jnp.expm1(-dt0))
    a_log = jnp.log(jax.random.uniform(ks[9], (DEPTH, 2, SSD_HEADS), f32, 1.0, 16.0))
    return {
        'x_prompt': nrm(ks[0], (BATCH, SEQ, D_MODEL), 1.0),
        'x_sample': nrm(ks[1], (DEC_BATCH, DEC_SEQ, D_MODEL), 1.0),
        'mem_prompt': nrm(ks[2], (BATCH, N_MEM, D_MODEL), 1.0),
        'mem_sample': nrm(ks[3], (DEC_BATCH, N_MEM, D_MODEL), 1.0),
        'norm_mix': gain(ks[4], (DEPTH, D_MODEL)),
        'w_in': nrm(ks[5], (DEPTH, D_MODEL, D_IN), D_MODEL ** -0.5),
        'conv_w': nrm(ks[6], (DEPTH, CONV_W, CONV_CH), CONV_W ** -0.5),
        'conv_b': nrm(ks[7], (DEPTH, CONV_CH), 0.02),
        'dt_bias': dt_bias,
        'a_log': a_log,
        'd_skip': 1.0 + nrm(ks[10], (DEPTH, SSD_HEADS), 0.1),
        'ssd_norm': gain(ks[11], (DEPTH, D_INNER)),
        'na_q_norm': gain(ks[12], (DEPTH, NA_HEAD_DIM)),
        'na_k_norm': gain(ks[13], (DEPTH, NA_HEAD_DIM)),
        'na_rpb': nrm(ks[14], (DEPTH, NA_HEADS, 2 * NA_MAX_KH - 1, 2 * NA_KW - 1), 0.1),
        'pool_w': nrm(ks[15], (DEPTH, POOL_GROUPS, POOL_GROUP_DIM, POOL_GROUP_DIM), POOL_GROUP_DIM ** -0.5),
        'pool_scale': gain(ks[16], (DEPTH, POOL_WIDTH)),
        'w_out': nrm(ks[17], (DEPTH, D_MIX, D_MODEL), D_MIX ** -0.5),
        'norm_xa': gain(ks[18], (DEPTH, D_MODEL)),
        'norm_mem': gain(ks[19], (DEPTH, D_MODEL)),
        'w_xq': nrm(ks[20], (DEPTH, D_MODEL, XA_WIDTH), D_MODEL ** -0.5),
        'w_xkv': nrm(ks[21], (DEPTH, D_MODEL, 2 * XA_WIDTH), D_MODEL ** -0.5),
        'xq_norm': gain(ks[22], (DEPTH, XA_HEAD_DIM)),
        'xk_norm': gain(ks[23], (DEPTH, XA_HEAD_DIM)),
        'w_xo': nrm(ks[24], (DEPTH, XA_WIDTH, D_MODEL), XA_WIDTH ** -0.5),
        'norm_ffn': gain(ks[25], (DEPTH, D_MODEL)),
        'w_router_group': nrm(ks[26], (DEPTH, D_MODEL, N_EXPERT_GROUPS), D_MODEL ** -0.5),
        'b_router_group': nrm(ks[27], (DEPTH, N_EXPERT_GROUPS), 0.01),
        'w_router_expert': nrm(ks[28], (DEPTH, D_MODEL, N_EXPERTS), D_MODEL ** -0.5),
        'b_router_expert': nrm(ks[29], (DEPTH, N_EXPERTS), 0.01),
        'w_e_gate': nrm(ks[30], (DEPTH, N_EXPERTS, D_MODEL, D_EXPERT), D_MODEL ** -0.5),
        'w_e_up': nrm(ks[31], (DEPTH, N_EXPERTS, D_MODEL, D_EXPERT), D_MODEL ** -0.5),
        'w_e_down': nrm(ks[32], (DEPTH, N_EXPERTS, D_EXPERT, D_MODEL), D_EXPERT ** -0.5),
    }

def reference(x_prompt, x_sample, mem_prompt, mem_sample, norm_mix, w_in, conv_w, conv_b, dt_bias, a_log, d_skip, ssd_norm, na_q_norm, na_k_norm, na_rpb, pool_w, pool_scale, w_out, norm_xa, norm_mem, w_xq, w_xkv, xq_norm, xk_norm, w_xo, norm_ffn, w_router_group, b_router_group, w_router_expert, b_router_expert, w_e_gate, w_e_up, w_e_down):
    layer_params = (norm_mix, w_in, conv_w, conv_b, dt_bias, a_log, d_skip, ssd_norm, na_q_norm, na_k_norm, na_rpb, pool_w, pool_scale, w_out, norm_xa, norm_mem, w_xq, w_xkv, xq_norm, xk_norm, w_xo, norm_ffn, w_router_group, b_router_group, w_router_expert, b_router_expert, w_e_gate, w_e_up, w_e_down)

    def trunk(x, mem):
        for layer in range(DEPTH):
            x = encoder_layer(x, mem, *[p[layer] for p in layer_params])
        return x

    y_prompt = trunk(x_prompt, mem_prompt)
    y_sample = trunk(x_sample, mem_sample)
    return (y_prompt, y_sample)


_drawn_inputs = setup_inputs


def setup_inputs(seed=0):
    import zlib

    import numpy as np

    out = dict(_drawn_inputs(seed))
    spreads = {}
    factors = {'ssd_norm': 2.807,
     'na_q_norm': 8.0,
     'na_k_norm': 8.0,
     'na_rpb': 4.14,
     'pool_scale': 3.572,
     'norm_xa': 8.0,
     'norm_mem': 5.915,
     'xq_norm': 8.0,
     'xk_norm': 8.0,
     'b_router_group': 34.576,
     'b_router_expert': 36.168,
     'norm_ffn': 8.0}
    for name, (base, spread) in spreads.items():
        noise = np.random.default_rng([zlib.crc32(name.encode()), seed]).standard_normal(out[name].shape)
        drawn = base * np.exp(spread * noise) if base else spread * noise
        out[name] = __import__('jax').numpy.asarray(drawn.astype(out[name].dtype))
    for name, factor in factors.items():
        out[name] = (out[name] * factor).astype(out[name].dtype)
    return out
```

```python
from contextlib import ExitStack

import concourse.bass as bass
import numpy as np
from concourse import mybir

F32 = mybir.dt.float32
F32R = mybir.dt.float32r
F16 = mybir.dt.float16
BF16 = mybir.dt.bfloat16
I32 = mybir.dt.int32
U32 = mybir.dt.uint32
ALU = mybir.AluOpType
ACT = mybir.ActivationFunctionType
AX_X = mybir.AxisListType.X

P = 128
D = 1024
KT = D // P
SEQS = 2
T = 512
TPS = T // P
NT = SEQS * TPS
EPS = 1e-6
NEG = -1e30

SSD_H, SSD_P, SSD_G, SSD_N = 8, 64, 2, 64
D_INNER = SSD_H * SSD_P
CONV_W = 4
GRID_W, ROWS = 64, 8
NA_H, NA_D, NA_KW = 4, 64, 16
RPB_R, RPB_C = 15, 31
POOL_D = 64
OFF_Z, OFF_XBC, OFF_DT = 0, 512, 1280
OFF_Q, OFF_V, OFF_U = 1296, 1808, 2064
N_MEM, XA_H, XA_D = 256, 4, 128
NG, EPG, NE = 4, 8, 32
DE = 256
NO = (2 * NT * P - 1) // P
NB = NE + NO

U_QK, U_V, U_BCU, U_XS, U_Z = range(5)
U_MK, U_MV, U_OUT0, U_OUT1, U_XQ, U_XO = range(10, 16)
N_RAW = 2
N_BANKS = 8
N_FIRST = 2
N_CONST = 8
N_INIT = 8
ROUND = 2.0 ** 23
R_STAGES = 5


def timeline():
    tl = []

    def mixed(main, *others):
        for group in spread(main, *others):
            tl.extend(group)

    def spread(main, *others):
        n, out = len(main), []
        for i, step in enumerate(main):
            out.append(list(step if isinstance(step, list) else [step]))
            for o in others:
                for x in o[len(o) * i // n:len(o) * (i + 1) // n]:
                    out[-1] += x if isinstance(x, list) else [x]
        return out

    def quarters(u):
        return [("w", u, q) for q in range(4)]

    for s in range(SEQS):
        t0 = s * TPS
        u0 = 5 * s
        tiles = range(t0, t0 + TPS)
        if s == 0:
            for i in tiles:
                tl += [("norm", "mix", i), ("w", U_QK, i), ("hT", "mix", i)] + ([("init",)] if i == 0 else [])
        dtv = [[("dtp", s)], [("vc", s, 0)], [("dtt", s), ("vt", s, 0), ("vc", s, 1)], [("vt", s, 1)]]
        main = spread(lagged("qk", tiles), quarters(u0 + U_V)) + spread(dtv, quarters(u0 + U_BCU))
        mixed(main, ssd_groups(s - 1) if s else [])
        conv, conv_t, u, u_t, na1, na2, nav = ([(kind, s, m) for m in range(n)] for kind, n in (
            ("conv", 6), ("convT", 5), ("u", 2), ("uT", 2), ("na1", 4), ("na2", 4), ("nav", 4)))
        mixed([[conv[4]], [u[0], na1[0]], [conv_t[4], conv[5]], [na2[0], u_t[0], u[1], nav[0]]],
              quarters(u0 + U_XS))
        mixed([[na1[1], conv[0]], [conv[1], conv_t[0], na2[1]]], quarters(u0 + U_Z))
        tl += [u_t[1], conv[2], nav[1], conv_t[1], na1[2], conv[3], conv_t[2]]
        st, nxt = ("mix", range(t0 + TPS, t0 + 2 * TPS)) if s == 0 else ("mem", range(4))
        z, norm, h_t = [("z", "z", i) for i in tiles], [("norm", st, i) for i in nxt], [("hT", st, i) for i in nxt]
        mixed([[norm[0], z[0], na2[2]], [h_t[0], norm[1], z[1], nav[2], na1[3], ("dtv", s)],
               [h_t[1], norm[2], z[2], ("dt", s), conv_t[3], na2[3]], [h_t[2], norm[3], z[3], ("sback", s, 3), nav[3]]],
              quarters(u0 + 5 if s == 0 else U_MK))
        tl += [h_t[3], ("sback", s, 2), ("gain", "xa" if s else "mem")]
    main = spread(lagged("mk", range(4)), quarters(U_MV))
    mv, mix_t = [("mv", "mv", i) for i in range(4)], [("mixT", "out", i) for i in range(NT)]
    main += spread([[mv[0]], [mv[1], mix_t[0]], [mv[2], mix_t[1]], [mv[3], mix_t[2]]], quarters(U_OUT0),
                   [("xld", i) for i in range(TPS)])
    main += spread([[("out", "out", i, 0)] + ([mix_t[3]] if i == 0 else []) for i in range(TPS)], quarters(U_OUT1))
    mixed(main, ssd_groups(1))
    tl += [("xld", i) for i in range(TPS, NT)]
    for i in range(TPS):
        tl += [("out", "out", i, 1), mix_t[TPS + i]]
    tl += [("out", "out", i, 0) for i in range(TPS, NT)]
    mixed([[("out", "out", TPS, 1), ("norm", "xa", 0)], [("out", "out", TPS + 1, 1), ("hT", "xa", 0), ("norm", "xa", 1)],
           ("out", "out", TPS + 2, 1), [("out", "out", TPS + 3, 1), ("hT", "xa", 1)]], quarters(U_XQ))
    tl += [("gain", "ffn")]
    for i in range(-2, NT + 2):
        def on(j, *steps):
            return list(steps) if 0 <= j < NT else []

        if i >= 1:
            tl += on(i + 2, ("norm", "xa", i + 2))
        tl += on(i, ("xs2", i))
        if i >= 0:
            tl += on(i + 2, ("hT", "xa", i + 2))
        tl += on(i + 1, ("hn3", "xq", i + 1))
        tl += on(i, ("xav", i))
        tl += on(i + 1, ("xs1", i + 1))
        tl += on(i + 2, ("hn1", "xq", i + 2), ("hn2", "xq", i + 2))
        if i == -1:
            tl.append(("norm", "xa", 2))
        if i < 0:
            tl += quarters(U_XO)[2 * i + 4:2 * i + 6]
        tl += on(i - 1, ("norm", "ffn", i - 1))
        tl += on(i, ("xo", i))
        tl += on(i - 1, ("hT", "ffn", i - 1), ("router", i - 1))
    return tl


def lagged(st, tiles):
    out = []
    for i in tiles:
        out.append([("hn1", st, i)] + ([("hn3", st, i - 1)] if i > tiles[0] else []) + [("hn2", st, i)])
    return out + [[("hn3", st, tiles[-1])]]


def ssd_groups(s):
    dec, y, out = ([(kind, s, c) for c in range(TPS)] for kind in ("sdec", "sy", "sout"))
    back = [[("sback", s, 1), dec[0]]]
    return back + [[y[0]], [dec[1], out[0]], [y[1]], [dec[2], out[1]], [y[2]], [dec[3], out[2]], [y[3]], [out[3]]]


def bank_uses(step):
    kind = step[0]
    if kind == "conv" or kind in ("vc", "vt", "dtp", "z", "mv", "hn1", "dt", "sback", "sout", "router", "dtt", "out"):
        return 1
    if kind == "hn3":
        return 1
    if kind == "u":
        return 1
    if kind == "uT":
        return 2
    if kind == "convT":
        return 1 if step[2] <= 4 else 0
    if kind == "hT":
        return 2
    if kind == "sdec":
        return 6
    if kind == "sy":
        return 4 if step[2] < TPS - 1 else 3
    if kind == "na1" or kind == "xs1":
        return 2
    if kind == "na2":
        return 2 if step[2] < 3 else 1
    if kind == "nav":
        return 1
    if kind == "xs2":
        return 2
    if kind == "xav":
        return 1
    if kind == "xo":
        return 2
    return 0


UNIT_OF = {"qk": U_QK, "z": U_Z, "mk": U_MK, "mv": U_MV, "xq": U_XQ}


class Plan:

    def __init__(self):
        self.tl = timeline()
        self.place = {}
        self.nth = {}
        seen = {}
        for step in self.tl:
            kind = step[0]
            self.nth[step] = seen.get(kind, 0)
            seen[kind] = self.nth[step] + 1
            for j in range(bank_uses(step)):
                n = len(self.place)
                self.place[step, j] = n
        self.use_at = {n: k for k, n in self.place.items()}
        self.free_no, count = {}, [0] * N_BANKS
        for n in range(len(self.place)):
            use = self.use_at[n]
            if self.own_release(*use) is None:
                count[n % N_BANKS] += 1
                self.free_no[use] = count[n % N_BANKS]
        self.raws = []
        for step in self.tl:
            if step[0] == "w":
                self.raws.append(step)
            elif step[0] == "norm" and step[1] in ("mix", "mem"):
                self.raws.append(step)
            elif step[0] == "mixT":
                self.raws.append(step)
        self.loads = [x for x in self.tl if x[0] == "xld" or x in self.raws]
        self.raw_no = {r: i for i, r in enumerate(self.raws)}
        self.ht = [x for x in self.tl if (x[0] == "hT" and x[1] != "ffn") or x[0] == "mixT"]
        self.ht_no = {x: i for i, x in enumerate(self.ht)}
        self.hs = [x for x in self.tl if x[0] == "hT" or x[0] == "mixT"]
        self.hs_no = {x: i for i, x in enumerate(self.hs)}

    def own_release(self, step, j):
        kind = step[0]
        if kind == "hT" and step[1] != "ffn":
            hs = [x for x in self.tl if (x[0] == "hT" and x[1] != "ffn") or x[0] == "mixT"]
            return "low", 2 * hs.index(step) + j + 1
        if kind == "out":
            return "x1", self.nth[step] + 1
        if kind == "conv":
            return "conv_sum", self.nth[step] + 1
        if kind == "z":
            return "zg_done", self.nth[step] + 1
        if kind == "xo":
            return "x2", 2 * self.nth[step] + j + 1
        if kind == "hn1":
            return "hnorm", self.nth[step] + 1
        if kind == "xav":
            return "o_low", self.nth[step] + 1
        return None

    def unit_last(self, u):
        if u < 10:
            s, k = divmod(u, 5)
            t = s * TPS + TPS - 1
            return {U_QK: ("hn1", "qk", t), U_V: ("vc", s, 1), U_BCU: ("u", s, 1), U_XS: ("conv", s, 3),
                    U_Z: ("z", "z", t)}[k]
        return {U_MK: ("hn1", "mk", 3), U_MV: ("mv", "mv", 3), U_OUT0: ("out", "out", NT - 1, 0),
                U_OUT1: ("out", "out", NT - 1, 1), U_XQ: ("hn1", "xq", NT - 1), U_XO: ("xo", NT - 1)}[u]

    def ht_last(self, use):
        st, i = use[1], use[2]
        return {"mix": ("z", "z", i), "mem": ("mv", "mv", i), "out": ("out", "out", i, 1), "xa": ("hn1", "xq", i)}[st]


def encoder_layer(nc, dram, out):
    plan = Plan()
    TL = plan.tl
    ctx = ExitStack()
    with ctx:
        def sem(name):
            return ctx.enter_context(nc.semaphore(name))

        bank = [ctx.enter_context(nc.psum_tensor(f"bank{b}", [P, 512], F32)) for b in range(N_BANKS)]

        mix_dram = nc.dram_tensor("mix_scratch", (NT, P, KT, P), F32).ap()
        z_dram = nc.dram_tensor("gate_scratch", (NT, P, D_INNER), F32).ap()
        hn_dram = nc.dram_tensor("ffn_rows", (NT * P, D), F32).ap()
        y_dram = nc.dram_tensor("expert_rows", (NE * P, D), F32).ap()
        yo_dram = nc.dram_tensor("further_rows", (NO * P, D), F32).ap()

        x_sb = ctx.enter_context(nc.sbuf_tensor("x_sb", [P, NT, D], F32))
        ident = ctx.enter_context(nc.sbuf_tensor("ident", [P, P], F32))
        logits = ctx.enter_context(nc.sbuf_tensor("logits", [P, NT, NG + NE], F32))
        stk = ExitStack()
        ctx.enter_context(stk)

        def sb(name, shape, dt=F32):
            return stk.enter_context(nc.sbuf_tensor(name, shape, dt))

        xfree = x_sb[:, :, :].rearrange("p a b -> p (a b)")
        taken = [0]

        def carve(*shape):
            n = int(np.prod(shape))
            v = xfree[:, taken[0]:taken[0] + n]
            taken[0] += n
            assert taken[0] <= NT * D
            if len(shape) == 2:
                v = v.rearrange("p (a b) -> p a b", a=shape[0])
            elif len(shape) == 3:
                v = v.rearrange("p (a b c) -> p a b c", a=shape[0], b=shape[1])
            return v

        qT = carve(2, T)
        kT = carve(2, T)
        v_sb = carve(TPS, NA_H * NA_D)
        cacc = carve(2, T)
        assert taken[0] == TPS * D
        xs = carve(TPS, D_INNER)
        bT = carve(T)
        cT = carve(T)
        btm = carve(TPS, P)
        zg = carve(D_INNER)

        Wh = [sb(f"Wh{i}", [P, 4096], F32R) for i in range(2)]
        Wl = [sb(f"Wl{i}", [P, 4096], F32R) for i in range(2)]
        raw = [sb(f"raw{i}", [P, 1024]) for i in range(N_RAW)]
        hTh = sb("hTh", [P, KT, T], F32R)
        hTl = sb("hTl", [P, KT, T], F32R)
        xn = sb("xn", [P, D])
        gain = sb("gain", [P, D])
        ssq = sb("ssq", [P, 64])
        ms = sb("ms", [P, 64])
        rs = sb("rs", [P, 64])
        sqb = sb("sqb", [P, 512])
        qn = sb("qn", [P, 512])
        hss = sb("hss", [P, 8])
        hms = sb("hms", [P, 8])
        hrs = sb("hrs", [P, 2, 8])
        prob = sb("prob", [P, 4, 256])
        probT = sb("probT", [P, 8, P])
        nmx = sb("nmx", [P, 4])
        mx = sb("mx", [P, 4])
        psm = sb("psm", [P, 4])
        prs = sb("prs", [P, 4])
        neghalf = sb("neghalf", [P, 16])
        y1 = sb("y1", [P, D_INNER])
        y2 = sb("y2", [P, D_INNER])
        tri_in = y2[:, 0:2 * P].rearrange("p (a b) -> p a b", a=2)
        mask = y2[:, 2 * P:2 * P + 32]
        tri_r = sb("tri_r", [P, 2, P], F32R)
        tri = tri_r[:, :, :].bitcast(F32)
        ones_r = sb("ones_r", [P, P], F32R)
        cols = sb("cols", [P, 40])
        cw, cb = cols[:, 0:24].rearrange("p (m j) -> p m j", m=6), cols[:, 24:30]
        p_scale, ssd_g, g_na, g_xa = cols[:, 30:32], cols[:, 32:36], cols[:, 36:38], cols[:, 38:40]
        rows = sb("rows", [P, 40])
        dt_bias, a_row, d_row = rows[:, 0:16], rows[:, 16:32], rows[:, 32:40]
        mix_stack = ExitStack()
        stk.enter_context(mix_stack)

        def sm(name, shape, dt=F32):
            return mix_stack.enter_context(nc.sbuf_tensor(name, shape, dt))

        nao = sm("nao", [P, 2, T])
        bias_in = sm("bias_in", [P, 2, 2, ROWS, 32])
        bias_ed = sm("bias_ed", [P, 2, 2, ROWS, 16])
        cth = sm("cth", [P, T])
        up = sm("up", [P, T + 16])
        wa = sm("wa", [P, T + 16])
        wb = sm("wb", [P, T + 16])
        cwh = sm("cwh", [P, 6, CONV_W])
        cbh = sm("cbh", [P, 6])
        pw_sb = sm("pw_sb", [P, 2, POOL_D])
        p_inv = sm("p_inv", [P, 2, 17])
        dtr = sm("dtr", [P, TPS, 16])
        dt1 = sm("dt1", [P, TPS, 16])
        dt2 = sm("dt2", [P, TPS, 16])
        dts = sm("dts", [P, TPS, 16])
        la = sm("la", [P, TPS, 16])
        laH = sm("laH", [P, TPS, 16], F32R)
        laL = sm("laL", [P, TPS, 16], F32R)
        cs = sm("cs", [P, 2, TPS, 8])
        tot = sm("tot", [P, TPS, 16])
        ncs = sm("ncs", [P, 2, TPS, 8])
        ecs = sm("ecs", [P, 2, TPS, 8])
        edec = sm("edec", [P, TPS, 16])
        wst = sm("wst", [P, 2, TPS, 8])
        dec = sm("dec", [P, 2, SSD_H, P])
        cbm = sm("cbm", [P, 2, 2, P])
        xdt = sm("xdt", [P, 2, D_INNER])
        xw = sm("xw", [P, D_INNER])
        S_f = sm("S_f", [P, D_INNER // 2])
        S_b = sm("S_b", [P, TPS - 1, D_INNER // 2])
        yss = sm("yss", [P, 2])
        yms = sm("yms", [P, 2])
        yrs = sm("yrs", [P, 2])
        mix_stack.close()
        xkT = sb("xkT", [P, XA_H, SEQS * N_MEM])
        xv = sb("xv", [P, 4, XA_H * XA_D])
        router_w = sb("router_ws", [P, KT, NG + NE])
        sb("apart", [P, 320])
        xqT = sb("xqT", [P, XA_H, P])
        oTh = sb("oTh", [P, XA_H * P], F32R)
        oTl = sb("oTl", [P, XA_H * P], F32R)
        hf = sb("hf", [P, KT, P])
        xn_ffn = sb("xn_ffn", [P, D])
        gain_ffn = sb("gain_ffn", [P, D])
        router_b = sb("router_b", [P, NG + NE])
        stk.close()
        NORMED = {"mix": (xn, gain), "mem": (xn, gain), "xa": (xn, gain), "ffn": (xn_ffn, gain_ffn)}

        def se(name, shape, dt=F32):
            return ctx.enter_context(nc.sbuf_tensor(name, shape, dt))

        WgH = [se(f"WgH{i}", [P, KT, 2 * DE], F32R) for i in range(2)]
        WgL = [se(f"WgL{i}", [P, KT, 2 * DE], F32R) for i in range(2)]
        WdH = [se(f"WdH{i}", [P, 2, D], F32R) for i in range(2)]
        WdL = [se(f"WdL{i}", [P, 2, D], F32R) for i in range(2)]
        eraw = [se(f"eraw{j}", [P, 1024]) for j in range(6)]
        xg = [se(f"xg{i}", [P, D]) for i in range(2)]
        xgH = [se(f"xgH{i}", [P, KT, P], F32R) for i in range(2)]
        xgL = [se(f"xgL{i}", [P, KT, P], F32R) for i in range(2)]
        eth = se("eth", [P, DE])
        ehb = se("ehb", [P, DE])
        hbH = se("hbH", [P, 2, P], F32R)
        hbL = se("hbL", [P, 2, P], F32R)
        ey = [se(f"ey{i}", [P, D]) for i in range(2)]
        idc = [se(f"idc{i}", [P, 1], U32) for i in range(2)]
        iota_e = se("iota_e", [P, NB + 1])
        iota_p = se("iota_p", [P, P])
        token0 = se("token0", [P, NT])
        token1 = se("token1", [P, NT])
        anchor = se("anchor", [P, 1])
        r_g = se("r_g", [P, NT, NG])
        r_g2 = se("r_g2", [P, NT, NG])
        r_e = se("r_e", [P, NT, NE])
        r_eq = se("r_eq", [P, NT, NE])
        oh = se("oh", [P, 2, NT, NE])
        r_max = se("r_max", [P, 3, NT])
        r_idx = se("r_idx", [P, 3, NT])
        gates = se("gates", [P, 2, NT])
        r_t = se("r_t", [P, 4, NT])
        cnt_b = se("cnt_b", [P, NT, NE], BF16)
        tri_b = se("tri_b", [P, P], BF16)
        ones_b = se("ones_b", [P, P], BF16)
        rank = se("rank", [P, NT, NE])
        n_e = se("n_e", [P, NE])
        ov = se("ov", [P, 4, NE])
        pos = se("pos", [P, 6, 2, NT])
        slot = se("slot", [P, 2, NT], U32)
        slot_o = se("slot_o", [P, 2, NT], U32)
        oneh_p = se("oneh_p", [P, 2 * NT, P], F16)
        oneh_b = se("oneh_b", [P, 2 * NT, NB + 1], F16)
        ids = se("ids", [P, NB + 1], U32)
        idt = se("idt", [P, NB + 1])
        r_both = ey[1][:, 0:2 * NT * NE].rearrange("p (c t e) -> p c t e", c=2, t=NT)
        ov3 = ey[0][:, 0:2 * NO * NE].rearrange("p (a b c) -> p a b c", a=2, b=NO)
        ovx = se("ovx", [P, NO])
        ovi = se("ovi", [P, NO + 1], I32)
        yg = [[eraw[0], eraw[1]], [eraw[2], eraw[3]]]

        r_pool = sem("r_pool")
        r_v = sem("r_v")
        r_a = sem("r_a")
        r_pe = sem("r_pe")
        eraw_full = [sem(f"eraw_full{j}") for j in range(6)]
        ew_high = sem("ew_high")
        ew_low = sem("ew_low")
        idc_done = sem("idc_done")
        anchored = sem("anchored")
        xg_ld = [sem(f"xg_ld{i}") for i in range(2)]
        xg_full = sem("xg_full")
        xg_high = sem("xg_high")
        xg_low = sem("xg_low")
        gu_full = sem("gu_full")
        th_done = sem("th_done")
        hb_done = sem("hb_done")
        hb_part = sem("hb_part")
        hb_full = sem("hb_full")
        hb_high = sem("hb_high")
        hb_low = sem("hb_low")
        y_full = sem("y_full")
        y_lo = sem("y_lo")
        y_hi = sem("y_hi")
        ey_st = [sem(f"ey_st{i}") for i in range(2)]
        yg_ld = [[sem(f"yg_ld{i}{c}") for c in range(2)] for i in range(2)]
        fill_st = sem("fill_st")
        yo_ld = sem("yo_ld")
        yg_used = sem("yg_used")
        out_st = sem("out_st")

        B_XG, B_GU, B_HB, B_Y, B_R = (0, 1), (2, 3), 4, (6, 7), 5
        GU_PIECES, PIECES = 4, 6

        def ew_parts(i):
            out = []
            for j, c in ((0, 0), (1, 0), (0, DE), (1, DE)):
                out.append(tuple(w[:, 4 * j:4 * j + 4, c:c + DE] for w in (WgH[i], WgL[i])))
            for a in range(2):
                out.append(tuple(w[:, a:a + 1, :] for w in (WdH[i], WdL[i])))
            return out

        def as_piece(v, j):
            return v[:, :].rearrange("p (k n) -> p k n", k=4 if j < GU_PIECES else 1)

        def pipeline(eng, step):
            step(1, 1, 0)
            step(2, 0, 0)
            with eng.Fori(1, NE // 2 - 2) as it:
                n = it * 2 + 1
                step(n, 1, it)
                step(n + 1, 0, it)
            step(NE - 3, 1, NE // 2 - 2)
            step(NE - 2, 0, NE // 2 - 2)
            step(NE - 1, 1, NE // 2 - 1)

        def further(eng, body):
            eng.wait_ge(r_v, R_STAGES + 1)
            count = eng.value_load(ovi[0:1, NO:NO + 1], min_val=0, max_val=NO)
            with eng.If(count > 0):
                with eng.Fori(0, NO) as b:
                    with eng.If(b < count):
                        body(b)

        full = [sem(f"bank_full{b}") for b in range(N_BANKS)]
        free = [sem(f"bank_free{b}") for b in range(N_BANKS)]
        raw_full = [sem(f"raw_full{i}") for i in range(N_RAW)]
        w_high = sem("w_high")
        w_low = sem("w_low")
        sq_done = sem("sq_done")
        rs_done = sem("rs_done")
        xn_done = sem("xn_done")
        high = sem("high")
        low = sem("low")
        x_ld = [sem(f"x_ld{s}") for s in range(SEQS)]
        x1 = sem("x1")
        x2 = sem("x2")
        hsq = sem("hsq")
        hsum = sem("hsum")
        hrms = sem("hrms")
        hnorm = sem("hnorm")
        first_ld = sem("first_ld")
        const_ld = sem("const_ld")
        init = sem("init")
        init_p = sem("init_p")
        init_a = sem("init_a")
        gain_ld = {st: sem(f"gain_ld_{st}") for st in ("mem", "xa", "ffn")}
        conv_sum = sem("conv_sum")
        conv_th = sem("conv_th")
        conv_out = sem("conv_out")
        zt_done = sem("zt_done")
        zg_done = sem("zg_done")
        z_st = [sem(f"z_st{i}") for i in range(NT)]
        z_ld = sem("z_ld")
        u_win = sem("u_win")
        ssd_st = [sem(f"ssd_st{s}") for s in range(SEQS)]
        nao_st = [sem(f"nao_st{s}") for s in range(SEQS)]
        po_st = [sem(f"po_st{s}") for s in range(SEQS)]
        dt_a = sem("dt_a")
        dt_v = sem("dt_v")
        s_chain = sem("dve_chain")
        p_chain = sem("pool_chain")
        a_chain = sem("act_chain")
        xw_done = sem("xw_done")
        xdt_done = sem("xdt_done")
        sf_done = sem("sf_done")
        e_done = sem("e_done")
        t_done = sem("t_done")
        y_done = sem("y_done")
        ysq_done = sem("ysq_done")
        yrs_done = sem("yrs_done")
        yn_done = sem("yn_done")
        max_done = sem("max_done")
        exp_done = sem("exp_done")
        prob_done = sem("prob_done")
        o_high = sem("o_high")
        o_low = sem("o_low")
        router_ld = sem("router_ld")
        hn_st = sem("hn_st")
        named = {"low": low, "x1": x1, "x2": x2, "hnorm": hnorm, "o_low": o_low, "conv_sum": conv_sum, "zg_done": zg_done}

        def pb(step, j=0):
            return bank[plan.place[step, j] % N_BANKS]

        def wait_full(eng, step, j=0):
            n = plan.place[step, j]
            eng.wait_ge(full[n % N_BANKS], n // N_BANKS + 1)

        def wait_released(eng, step, j=0):
            own = plan.own_release(step, j)
            if own:
                eng.wait_ge(named[own[0]], own[1])
            else:
                n = plan.place[step, j]
                eng.wait_ge(free[n % N_BANKS], plan.free_no[step, j])

        def take(pe, step, j=0):
            n = plan.place[step, j]
            if n >= N_BANKS:
                wait_released(pe, *plan.use_at[n - N_BANKS])
            return bank[n % N_BANKS]

        def is_full(step, j=0):
            return full[plan.place[step, j] % N_BANKS]

        def is_free(step, j=0):
            return free[plan.place[step, j] % N_BANKS]

        def raw_of(step):
            return raw[plan.raw_no[step] % N_RAW]

        def wait_raw(eng, step):
            r = plan.raw_no[step]
            eng.wait_ge(raw_full[r % N_RAW], 32 * (r // N_RAW + 1))

        def ht_cols(step):
            i = plan.ht_no[step] % TPS
            return slice(i * P, (i + 1) * P)

        def unit_w(u):
            return Wh[u % 2], Wl[u % 2]

        def nth(*step):
            return plan.nth[step]

        softmaxes = [x for x in TL if x[0] in ("na1", "xs1")]
        head_norms = [x for x in TL if x[0] == "hn1"]
        transposed = [x for x in TL if x[0] == "hT"]

        def softmax_step(s, m):
            return ("xs1", m) if s == 2 else ("na1", s, m)

        def sm_no(s, m):
            return softmaxes.index(softmax_step(s, m))

        def xw_no(s, backward, c):
            return 6 * s + (TPS - 1 - c if backward else TPS - 1 + c)

        def second_step(k):
            x = softmaxes[k]
            return ("xs2", x[1]) if x[0] == "xs1" else ("na2",) + x[1:]

        def prob_banks(x):
            return bank_uses(x)

        def wait_transposed(eng, k):
            if k:
                x = second_step(k - 1)
                for half in range(prob_banks(x)):
                    wait_full(eng, x, half)

        conv_steps = [x for x in TL if x[0] == "conv"]
        uses_u = [x[1:] for x in TL if x[0] == "u"]

        def decayed(pool, s, dr, c, per_head, heads):
            if dr:
                if (s, c) != (0, TPS - 1):
                    prev = ("sback", s, c + 1) if c < TPS - 1 else ("sy", s - 1, TPS - 2)
                    wait_full(pool, prev, 3 if prev[0] == "sy" else 0)
            else:
                prev = ("sy", s, c - 1) if c else ("sback", s, 1)
                wait_full(pool, prev, 3 if prev[0] == "sy" else 0)
            pool.tensor_tensor(heads(xw[:, :]), heads(xs[:, c, :]), per_head(wst[:, dr, c, :], SSD_P), ALU.mult)\
                .then_inc(xw_done, 1)

        def wait_na_pool(eng):
            eng.wait_ge(nao_st[SEQS - 1], 16 * 2)
            eng.wait_ge(po_st[SEQS - 1], 16 * 2)

        def wait_mixed(eng):
            eng.wait_ge(ssd_st[SEQS - 1], 16 * TPS)
            eng.wait_ge(nao_st[SEQS - 1], 16 * 2)
            eng.wait_ge(po_st[SEQS - 1], 16 * 2)

        chunks = [(s, c) for s in range(SEQS) for c in range(TPS)]

        def before(kind, step):
            return sum(x[0] == kind for x in TL[:TL.index(step)])

        HN_GROUPS = {"qk": (8, 64), "mk": (4, 128), "xq": (4, 128)}
        STEP_UNIT = {"qk": U_QK, "z": U_Z}

        def unit_for(st, i):
            if st in STEP_UNIT:
                return 5 * (i // TPS) + STEP_UNIT[st]
            return UNIT_OF[st]

        HT_STAGE = {"qk": "mix", "z": "mix", "mk": "mem", "mv": "mem", "xq": "xa"}

        def col_range(u):
            if u < 10:
                return {U_QK: ("w_in", OFF_Q, 512), U_V: ("w_in", OFF_V, 256), U_XS: ("w_in", OFF_XBC, 512),
                        U_Z: ("w_in", OFF_Z, 512)}[u % 5]
            return {U_MK: ("w_xkv", 0, 512), U_MV: ("w_xkv", 512, 512), U_OUT0: ("w_out", 0, 512),
                    U_OUT1: ("w_out", 512, 512), U_XQ: ("w_xq", 0, 512)}[u]

        block = ctx.enter_context(nc.Block())

        @block.sync
        def _(sp):
            def released_raw(r):
                step = plan.raws[r]
                if step[0] == "w":
                    sp.wait_ge(w_low, 1 + nth(*step))
                elif step[0] == "norm":
                    sp.wait_ge(xn_done, 1 + nth(*step))
                else:
                    sp.wait_ge(low, 2 * plan.ht_no[step] + 2)

            for step in plan.loads:
                if step[0] == "xld":
                    i = step[1]
                    if i == 0:
                        wait_released(sp, ("nav", 1, 3))
                        wait_released(sp, ("convT", 1, 3))
                    elif i == TPS:
                        sp.wait_ge(ssd_st[SEQS - 1], 16 * TPS)
                    sp.dma_start(x_sb[:, i, :], dram["x"][i // TPS][0][(i % TPS) * P:(i % TPS + 1) * P, :])\
                        .then_inc(x_ld[i // TPS], 16)
                    continue
                r = plan.raw_no[step]
                slot = raw[r % N_RAW]
                if r >= N_RAW:
                    released_raw(r - N_RAW)
                done = raw_full[r % N_RAW]
                if step[0] == "w":
                    u, q = step[1], step[2]
                    if u < 10 and u % 5 == U_BCU:
                        w = dram["w_in"][0][2 * q * P:(2 * q + 2) * P, :].rearrange("(k p) n -> p k n", p=P)
                        v = slot[:, :].rearrange("p (k n) -> p k n", k=2)
                        c = OFF_XBC + D_INNER
                        sp.dma_start(v[:, :, 0:256], w[:, :, c:c + 256]).then_inc(done, 16)
                        sp.dma_start(v[:, :, 256:512], w[:, :, OFF_U:OFF_U + 256]).then_inc(done, 16)
                    elif u < 10 and u % 5 == U_V:
                        w = dram["w_in"][0][2 * q * P:(2 * q + 2) * P, :].rearrange("(k p) n -> p k n", p=P)
                        v = slot[:, :].rearrange("p (k n) -> p k n", k=2)
                        sp.dma_start(v[:, :, 0:256], w[:, :, OFF_V:OFF_V + 256]).then_inc(done, 16)
                        sp.dma_start(v[:, :, 256:272], w[:, :, OFF_DT:OFF_DT + 16]).then_inc(done, 16)
                    elif u == U_XO:
                        for a in range(2):
                            sp.dma_start(slot[:, a * 512:(a + 1) * 512],
                                         dram["w_xo"][0][q * P:(q + 1) * P, a * 512:(a + 1) * 512]).then_inc(done, 16)
                    else:
                        name, c0, n = col_range(u)
                        for a in range(2):
                            k = 2 * q + a
                            sp.dma_start(slot[:, a * 512:(a + 1) * 512],
                                         dram[name][0][k * P:(k + 1) * P, c0:c0 + n]).then_inc(done, 16)
                else:
                    i = step[2]
                    if step[0] == "mixT":
                        if i % TPS == 0:
                            sp.wait_ge(ssd_st[i // TPS], 16 * TPS)
                            sp.wait_ge(nao_st[i // TPS], 16 * 2)
                            sp.wait_ge(po_st[i // TPS], 16 * 2)
                        src = mix_dram[i].rearrange("p k t -> p (k t)")
                    elif step[0] == "norm" and step[1] == "mem":
                        src = dram["mem"][i // 2][0][(i % 2) * P:(i % 2 + 1) * P, :]
                    else:
                        src = dram["x"][i // TPS][0][(i % TPS) * P:(i % TPS + 1) * P, :]
                    for a in range(2):
                        sp.dma_start(slot[:, a * 512:(a + 1) * 512], src[:, a * 512:(a + 1) * 512]).then_inc(done, 16)

            wait_released(sp, ("router", NT - 1))
            sp.wait_ge(hn_st, 16 * NT)
            e_src = [dram[w][0].rearrange("e (p k) n -> e p (k n)", p=P) for w in ("w_e_gate", "w_e_up", "w_e_down")]

            def load_piece(e, j):
                src = e_src[j // 2][bass.ds(e, 1), :, (j % 2) * 1024:(j % 2) * 1024 + 1024]
                sp.dma_start(eraw[j][:, :], src.rearrange("o p n -> (o p) n")).then_inc(eraw_full[j], 16)

            for j in range(PIECES):
                load_piece(0, j)

            with sp.Fori(1, NE) as e:
                need = [sp.snap(e * PIECES - (PIECES - 1 - j)) for j in range(PIECES)]
                for j in range(PIECES):
                    sp.wait_ge(ew_low, need[j])
                    load_piece(e, j)

            def more(b):
                e = sp.value_load(ovi[0:1, bass.ds(b, 1)], min_val=0, max_val=NE - 1)
                sp.wait_ge(ew_low, b * PIECES + PIECES * NE)
                for j in range(PIECES):
                    load_piece(e, j)

            further(sp, more)

            for i in range(NT):
                sp.wait_ge(yg_used, 2 * i + 2)
                sp.dma_start(out[i // TPS][0][(i % TPS) * P:(i % TPS + 1) * P, :], x_sb[:, i, :]).then_inc(out_st, 16)
            sp.wait_ge(out_st, 16 * NT)

        @block.tensor
        def _(pe):
            def three(dst, ah, al, bh, bl, first, last):
                pe.matmul(dst, ah, bh, start=first, stop=False)
                pe.matmul(dst, ah, bl, start=False, stop=False)
                return pe.matmul(dst, al, bh, start=False, stop=last)

            def wait_ht(st, i):
                step = ("mixT", st, i) if st == "out" else ("hT", st, i)
                pe.wait_ge(low, 2 * plan.ht_no[step] + 2)
                return ht_cols(step)

            def wait_unit(u):
                pe.wait_ge(w_low, 1 + nth("w", u, 3))

            def tokens_by_weights(step, st, i, n=512):
                c = wait_ht(HT_STAGE[st], i)
                u = unit_for(st, i)
                wait_unit(u)
                wh, wl = unit_w(u)
                b = take(pe, step)
                for k in range(KT):
                    last = three(b[:, 0:n], hTh[:, k, c], hTl[:, k, c], wh[:, k * 512:k * 512 + n],
                                 wl[:, k * 512:k * 512 + n], k == 0, k == KT - 1)
                last.then_inc(is_full(step), 1)

            def channels_by_tokens(step, s, u, c0, m=P):
                wait_ht("mix", s * TPS + TPS - 1)
                wait_unit(u)
                wh, wl = unit_w(u)
                b = take(pe, step)
                for k in range(KT):
                    w = slice(k * 512 + c0, k * 512 + c0 + m)
                    last = three(b[0:m, :], wh[:, w], wl[:, w], hTh[:, k, :], hTl[:, k, :], k == 0, k == KT - 1)
                last.then_inc(is_full(step), 1)

            pe.wait_ge(first_ld, 16 * N_FIRST)
            for step in TL:
                kind = step[0]
                if kind == "init":
                    pe.wait_ge(const_ld, 16 * N_CONST)
                    pe.wait_ge(init, N_INIT)
                    pe.wait_ge(init_p, 2)
                if kind == "hT":
                    st, i = step[1], step[2]
                    pe.wait_ge(xn_done, 1 + nth("norm", st, i))
                    for half in range(2):
                        b = take(pe, step, half)
                        for j in range(4):
                            f = 4 * half + j
                            last = pe.transpose(b[:, j * P:(j + 1) * P], NORMED[st][0][:, f * P:(f + 1) * P],
                                                ident[:, :])
                        last.then_inc(is_full(step, half), 1)
                elif kind == "hn1":
                    tokens_by_weights(step, step[1], step[2])
                elif kind in ("z", "mv"):
                    tokens_by_weights(step, kind, step[2])
                elif kind == "hn3":
                    pe.wait_ge(hnorm, 1 + nth(*step))
                    b = take(pe, step)
                    for j in range(4):
                        last = pe.transpose(b[:, j * P:(j + 1) * P], qn[:, j * P:(j + 1) * P], ident[:, :])
                    last.then_inc(is_full(step), 1)
                elif kind == "vc":
                    s, m = step[1], step[2]
                    channels_by_tokens(step, s, 5 * s + U_V, m * P)
                elif kind == "dtp":
                    channels_by_tokens(step, step[1], 5 * step[1] + U_V, 256, 16)
                elif kind == "dtt":
                    wait_released(pe, ("dtp", step[1]))
                    b = take(pe, step)
                    for c in range(TPS):
                        last = pe.transpose(b[:, c * 16:(c + 1) * 16], cth[0:16, c * P:(c + 1) * P],
                                            ident[0:16, 0:16])
                    last.then_inc(is_full(step), 1)
                elif kind == "vt":
                    wait_released(pe, ("vc",) + step[1:])
                    b = take(pe, step)
                    for c in range(TPS):
                        last = pe.transpose(b[:, c * P:(c + 1) * P], qn[:, c * P:(c + 1) * P], ident[:, :])
                    last.then_inc(is_full(step), 1)
                elif kind == "conv":
                    s, m = step[1], step[2]
                    u = 5 * s + (U_XS if m < 4 else U_BCU)
                    channels_by_tokens(step, s, u, (m % 4) * P)
                elif kind == "convT" and step[2] <= 4:
                    s, m = step[1], step[2]
                    pe.wait_ge(conv_out, 1 + nth("conv", s, m))
                    src = cacc[:, nth("conv", s, m) % 2, :] if m < 4 else bT[:, :]
                    b = take(pe, step)
                    for c in range(TPS):
                        last = pe.transpose(b[:, c * P:(c + 1) * P], src[:, c * P:(c + 1) * P], ident[:, :])
                    last.then_inc(is_full(step), 1)
                elif kind == "u":
                    s, m = step[1], step[2]
                    channels_by_tokens(step, s, 5 * s + U_BCU, 256 + m * P)
                elif kind == "uT":
                    m = step[2]
                    pe.wait_ge(u_win, 1 + nth(*step))
                    for j in range(2):
                        b = take(pe, step, j)
                        r = slice(64 * j, 64 * j + 64)
                        pe.matmul(b[r, :], pw_sb[r, m, :], up[r, 8:T + 8], start=True, stop=True)\
                            .then_inc(is_full(step, j), 1)
                elif kind == "dt":
                    pe.wait_ge(dt_v, 4 * nth(*step) + 2)
                    b = take(pe, step)
                    for dr in range(2):
                        for j, a in enumerate((laH, laL)):
                            pe.matmul(b[:, dr * 32:dr * 32 + 32].rearrange("p (c h) -> p c h", c=TPS),
                                      tri_r[:, dr, :], a[:, :, dr * 8:dr * 8 + 8], start=j == 0, stop=j == 1)
                    for j, a in enumerate((laH, laL)):
                        last = pe.matmul(b[:, 64:128], ones_r[:, :], a[:, :, :].rearrange("p c h -> p (c h)"),
                                         start=j == 0, stop=j == 1)
                    last.then_inc(is_full(step), 1)
                elif kind == "sback":
                    s, c = step[1], step[2]
                    wait_released(pe, ("convT", s, 4))
                    pe.wait_ge(xw_done, 1 + xw_no(s, 1, c))
                    b = take(pe, step)
                    pe.matmul(b[:, :], btm[:, c, :], xw[:, :], start=True, stop=True).then_inc(is_full(step), 1)
                elif kind == "sdec":
                    s, c = step[1], step[2]
                    tok = slice(c * P, (c + 1) * P)
                    pe.wait_ge(conv_out, 1 + max(nth("conv", s, 4), nth("conv", s, 5)))
                    for g in range(SSD_G):
                        b = take(pe, step, g)
                        r = slice(64 * g, 64 * g + 64)
                        pe.matmul(b[:, 0:P], bT[r, tok], cT[r, tok], start=True, stop=True)\
                            .then_inc(is_full(step, g), 1)
                    for dr in range(2):
                        for hh in range(2):
                            b = take(pe, step, 2 + 2 * dr + hh)
                            for h in range(4):
                                e = dr * 8 + hh * 4 + h
                                for j, a in enumerate((laH, laL)):
                                    last = pe.matmul(b[:, h * P:(h + 1) * P], a[:, c, e:e + 1].to_broadcast([P, P]),
                                                     tri_r[:, dr, :], start=j == 0, stop=j == 1)
                            last.then_inc(is_full(step, 2 + 2 * dr + hh), 1)
                elif kind == "sy":
                    s, c = step[1], step[2]
                    tok = slice(c * P, (c + 1) * P)
                    if c:
                        wait_released(pe, ("sy", s, c - 1), 3)
                    else:
                        pe.wait_ge(sf_done, s + 1)
                    if c < TPS - 1:
                        wait_released(pe, ("sback", s, c + 1))
                    for g in range(SSD_G):
                        b = take(pe, step, 1 + g)
                        r = slice(64 * g, 64 * g + 64)
                        last = pe.matmul(b[:, 0:256], cT[r, tok], S_f[r, :], start=True, stop=True)
                        if c < TPS - 1:
                            last = pe.matmul(b[:, 256:512], cT[r, tok], S_b[r, c, :], start=True, stop=True)
                        last.then_inc(is_full(step, 1 + g), 1)
                    if c < TPS - 1:
                        pe.wait_ge(xw_done, 1 + xw_no(s, 0, c))
                        b = take(pe, step, 3)
                        pe.matmul(b[:, :], btm[:, c, :], xw[:, :], start=True, stop=True)\
                            .then_inc(is_full(step, 3), 1)
                    pe.wait_ge(t_done, 1 + nth("sdec", s, c))
                    pe.wait_ge(xdt_done, 1 + nth("sdec", s, c))
                    b = take(pe, step, 0)
                    for h in range(SSD_H):
                        hc = slice(h * SSD_P, (h + 1) * SSD_P)
                        for dr in range(2):
                            last = pe.matmul(b[:, hc], dec[:, dr, h, :], xdt[:, dr, hc], start=dr == 0, stop=dr == 1)
                    last.then_inc(is_full(step, 0), 1)
                elif kind == "sout":
                    pe.wait_ge(yn_done, 1 + nth(*step))
                    b = take(pe, step)
                    for j in range(4):
                        last = pe.transpose(b[:, j * P:(j + 1) * P], y2[:, j * P:(j + 1) * P], ident[:, :])
                    last.then_inc(is_full(step), 1)
                elif kind == "na1":
                    s, m = step[1], step[2]
                    for i in range(s * TPS, s * TPS + TPS):
                        wait_released(pe, ("hn3", "qk", i))
                    for par in range(2):
                        b = take(pe, step, par)
                        r = slice(64 * par, 64 * par + 64)
                        for pair in range(2):
                            qv = qT[r, pair, :]
                            kv = kT[r, pair, :].rearrange("p (r c) -> p r c", r=ROWS)
                            if m < 3:
                                keys = kv[:, :, 16 * m:16 * m + 32].rearrange("p r (b c) -> p b r c", b=2)
                                last = pe.matmul(b[:, pair * 256:pair * 256 + 256], qv[:, m * P:(m + 1) * P], keys,
                                                 start=True, stop=True)
                            else:
                                for side in range(2):
                                    last = pe.matmul(b[64 * side:64 * side + 64, pair * 128:pair * 128 + 128],
                                                     qv[:, 384 + 64 * side:448 + 64 * side],
                                                     kv[:, :, 48 * side:48 * side + 16], start=True, stop=True)
                        last.then_inc(is_full(step, par), 1)
                elif kind == "na2":
                    s, m = step[1], step[2]
                    wait_released(pe, ("vt", s, 1))
                    pe.wait_ge(prob_done, 1 + sm_no(s, m))
                    n_bk = 2 if m < 3 else 1
                    for half in range(n_bk):
                        b = take(pe, step, half)
                        for j in range(4):
                            if m < 3:
                                h, blk = divmod(4 * half + j, 2)
                                src = prob[:, h, blk * P:(blk + 1) * P]
                            else:
                                src = prob[:, j, 0:P]
                            last = pe.transpose(b[:, j * P:(j + 1) * P], src, ident[:, :])
                        last.then_inc(is_full(step, half), 1)
                elif kind == "nav":
                    s, m = step[1], step[2]
                    for half in range(2 if m < 3 else 1):
                        wait_released(pe, ("na2", s, m), half)
                    b = take(pe, step)
                    for par in range(2):
                        r = slice(64 * par, 64 * par + 64)
                        for pair in range(2):
                            h = 2 * pair + par
                            hc = slice(h * 64, h * 64 + 64)
                            if m < 3:
                                for blk in range(2):
                                    last = pe.matmul(b[r, pair * P:pair * P + P], v_sb[:, m + blk, hc],
                                                     probT[:, (2 * par + pair) * 2 + blk, :],
                                                     start=blk == 0, stop=blk == 1)
                            else:
                                for side in range(2):
                                    last = pe.matmul(b[r, pair * P + 64 * side:pair * P + 64 * side + 64],
                                                     v_sb[:, 3 * side, hc],
                                                     probT[:, 2 * par + pair, 64 * side:64 * side + 64],
                                                     start=True, stop=True)
                    last.then_inc(is_full(step), 1)
                elif kind == "out":
                    i, half = step[2:]
                    c = wait_ht("out", i)
                    u = U_OUT0 + half
                    wait_unit(u)
                    wh, wl = unit_w(u)
                    b = take(pe, step)
                    for k in range(KT):
                        w = slice(k * 512, (k + 1) * 512)
                        last = three(b[:, :], hTh[:, k, c], hTl[:, k, c], wh[:, w], wl[:, w], k == 0, k == KT - 1)
                    last.then_inc(is_full(step), 1)
                elif kind == "xs1":
                    i = step[1]
                    s = i // TPS
                    wait_released(pe, ("hn3", "xq", i))
                    if i == 0:
                        wait_released(pe, ("hn3", "mk", 3))
                    for half in range(2):
                        b = take(pe, step, half)
                        for j in range(2):
                            h = 2 * half + j
                            last = pe.matmul(b[:, j * 256:(j + 1) * 256], xqT[:, h, :],
                                             xkT[:, h, s * N_MEM:(s + 1) * N_MEM], start=True, stop=True)
                        last.then_inc(is_full(step, half), 1)
                elif kind == "xs2":
                    i = step[1]
                    pe.wait_ge(prob_done, 1 + sm_no(2, i))
                    for half in range(2):
                        b = take(pe, step, half)
                        for j in range(4):
                            h, kt = divmod(4 * half + j, 2)
                            last = pe.transpose(b[:, j * P:(j + 1) * P], prob[:, h, kt * P:(kt + 1) * P], ident[:, :])
                        last.then_inc(is_full(step, half), 1)
                elif kind == "xav":
                    i = step[1]
                    s = i // TPS
                    for half in range(2):
                        wait_released(pe, ("xs2", i), half)
                    if i == 0:
                        wait_released(pe, ("mv", "mv", 3))
                    b = take(pe, step)
                    for h in range(XA_H):
                        for kt in range(2):
                            last = pe.matmul(b[:, h * P:(h + 1) * P], xv[:, 2 * s + kt, h * P:(h + 1) * P],
                                             probT[:, 2 * h + kt, :], start=kt == 0, stop=kt == 1)
                    last.then_inc(is_full(step), 1)
                elif kind == "xo":
                    i = step[1]
                    pe.wait_ge(o_low, i + 1)
                    wait_unit(U_XO)
                    wh, wl = unit_w(U_XO)
                    for half in range(2):
                        b = take(pe, step, half)
                        for h in range(XA_H):
                            w = slice(h * 1024 + half * 512, h * 1024 + half * 512 + 512)
                            last = three(b[:, :], oTh[:, h * P:(h + 1) * P], oTl[:, h * P:(h + 1) * P], wh[:, w],
                                         wl[:, w], h == 0, h == XA_H - 1)
                        last.then_inc(is_full(step, half), 1)
                elif kind == "router":
                    i = step[1]
                    pe.wait_ge(router_ld, 64)
                    for half in range(2):
                        wait_released(pe, ("hT", "ffn", i), half)
                    b = take(pe, step)
                    for k in range(KT):
                        last = pe.matmul(b[:, 0:NG + NE], hf[:, k, :], router_w[:, k, :], start=k == 0,
                                         stop=k == KT - 1)
                    last.then_inc(is_full(step), 1)

            for n in range(len(plan.place) - N_BANKS, len(plan.place)):
                wait_released(pe, *plan.use_at[n])
            pe.wait_ge(r_v, 3)
            b = bank[B_R]
            pe.matmul(b[:, 0:NT * NE], tri_b[:, :], cnt_b[:, :, :].rearrange("p a b -> p (a b)"), start=True, stop=False)
            for i in range(1, NT):
                to = b[:, i * NE:NT * NE].rearrange("p (a b) -> p a b", b=NE)
                pe.matmul(to, ones_b[:, :], cnt_b[:, i - 1, :].unsqueeze(1).to_broadcast([P, NT - i, NE]),
                          start=False, stop=i == NT - 1)
            for i in range(NT):
                last = pe.matmul(b[:, NT * NE:NT * NE + NE], ones_b[:, :], cnt_b[:, i, :], start=i == 0, stop=i == NT - 1)
            last.then_inc(r_pe, 1)
            pe.wait_ge(r_v, 4)
            b = bank[B_HB]
            for j in range(2 * NT):
                last = pe.matmul(b[:, 0:NB + 1], oneh_p[:, j, :], oneh_b[:, j, :], start=j == 0, stop=j == 2 * NT - 1)
            last.then_inc(r_pe, 1)
            pe.wait_ge(r_v, R_STAGES)

            def turn_rows(n, i, loads):
                pe.wait_ge(xg_ld[i], 16 * loads)
                if not isinstance(n, int) or n > 0:
                    pe.wait_ge(xg_low, 2 * n)
                for half in range(2):
                    b = bank[B_XG[half]]
                    for j in range(4):
                        k = 4 * half + j
                        last = pe.transpose(b[:, j * P:(j + 1) * P], xg[i][:, k:D:KT], ident[:, :])
                    last.then_inc(xg_full, 1)

            def gate_up(n, i):
                pe.wait_ge(xg_low, 2 * n + 2)
                pe.wait_ge(ew_low, PIECES * n + GU_PIECES)
                if not isinstance(n, int) or n > 1:
                    pe.wait_ge(hb_done, n - 1)
                b = bank[B_GU[i]]
                for k in range(KT):
                    last = three(b[:, :], xgH[i][:, k, :], xgL[i][:, k, :], WgH[i][:, k, :], WgL[i][:, k, :], k == 0,
                                 k == KT - 1)
                last.then_inc(gu_full, 1)

            def turn_hidden(n):
                pe.wait_ge(hb_done, n + 1)
                if not isinstance(n, int) or n > 0:
                    pe.wait_ge(hb_low, n)
                b = bank[B_HB]
                for k in range(2):
                    last = pe.transpose(b[:, k * P:(k + 1) * P], ehb[:, k:DE:2], ident[:, :])
                last.then_inc(hb_full, 1)

            def down(n, i):
                pe.wait_ge(hb_low, n + 1)
                pe.wait_ge(ew_low, PIECES * n + PIECES)
                for half in range(2):
                    if not isinstance(n, int) or n > 0:
                        pe.wait_ge(y_hi if half else y_lo, n)
                    b = bank[B_Y[half]]
                    c = slice(half * 512, half * 512 + 512)
                    for k in range(2):
                        last = three(b[:, :], hbH[:, k, :], hbL[:, k, :], WdH[i][:, k, c], WdL[i][:, k, c], k == 0,
                                     k == 1)
                    last.then_inc(y_full, 1)

            turn_rows(0, 0, 1)
            turn_rows(1, 1, 1)
            gate_up(0, 0)

            def step(n, i, it):
                turn_hidden(n - 1)
                if not (isinstance(n, int) and n == NE - 1):
                    turn_rows(n + 1, 1 - i, it + 2)
                gate_up(n, i)
                down(n - 1, 1 - i)

            pipeline(pe, step)
            turn_hidden(NE - 1)
            down(NE - 1, 1)

            def more(b):
                turn_rows(b + NE, 0, b + NE // 2 + 1)
                gate_up(b + NE, 0)
                turn_hidden(b + NE)
                down(b + NE, 0)

            further(pe, more)

        @block.scalar
        def _(act):
            chain = [0]

            def link(ins):
                chain[0] += 1
                ins.then_inc(a_chain, 1)
                act.wait_ge(a_chain, chain[0])

            n = [0]

            def load(dst, src):
                act.dma_start(dst, src).then_inc(first_ld if n[0] < N_FIRST else const_ld, 16)
                n[0] += 1

            def row(ap, count, offset=0):
                return bass.AP(ap.tensor, offset, [[0, P], [1, count]])

            load(ident[:, :], dram["c_ident"])
            load(gain[:, :], row(dram["norm_mix"], D))
            load(tri_in, dram["c_tri"].rearrange("a p n -> p a n"))
            load(cols[:, :], dram["l_cols"])
            load(rows[:, :], row(dram["l_rows"], 40))
            load(pw_sb[:, :, :], dram["pool_w"][0].rearrange("(m g) c d -> (g c) m d", g=2))
            load(p_inv[:, :, :], dram["c_inv"])
            load(bias_in[:, :, :, :, :], dram["l_bias_in"])
            load(bias_ed[:, :, :, :, :], dram["l_bias_ed"])
            load(mask, dram["c_mask"])
            assert n[0] == N_FIRST + N_CONST

            def copy(dst, src, **kw):
                return act.activation(dst, src, ACT.Copy, **kw)

            for step in TL:
                kind = step[0]
                if kind == "init":
                    act.wait_ge(const_ld, 16 * N_CONST)
                    act.activation(a_row[:, :], a_row[:, :], ACT.Exp).then_inc(init_a, 1)
                elif kind == "w":
                    u, q = step[1], step[2]
                    wait_raw(act, step)
                    if u >= 2:
                        prev = plan.unit_last(u - 2)
                        wait_full(act, prev, bank_uses(prev) - 1)
                    wh, _wl = unit_w(u)
                    src, dst = raw_of(step), wh
                    if u < 10 and u % 5 == U_V:
                        copy(wh[:, q * 1024:(q + 1) * 1024].rearrange("p (k n) -> p k n", k=2)[:, :, 0:272],
                             src[:, :].rearrange("p (k n) -> p k n", k=2)[:, :, 0:272]).then_inc(w_high, 1)
                    else:
                        copy(wh[:, q * 1024:(q + 1) * 1024], src[:, :]).then_inc(w_high, 1)
                elif kind == "norm":
                    st, i = step[1], step[2]
                    k = nth(*step)
                    if k and not (st == "ffn" and i == 0):
                        wait_full(act, [x for x in transposed if (x[1] == "ffn") == (st == "ffn")
                                        and TL.index(x) < TL.index(step)][-1], 1)
                    if st == "ffn" and i:
                        act.wait_ge(hn_st, 16 * i)
                    if st in ("mix", "mem"):
                        wait_raw(act, step)
                        src = raw_of(step)[:, :]
                    else:
                        if st == "xa":
                            act.wait_ge(x1, 1 + max(nth("out", "out", i, half) for half in range(2)))
                        else:
                            act.wait_ge(x2, 2 * i + 2)
                        src = x_sb[:, i, :]
                    act.activation(NORMED[st][0][:, :], src, ACT.Square, accum_out=ssq[:, k:k + 1]).then_inc(sq_done, 1)
                elif kind == "hT" and step[1] == "ffn":
                    i = step[2]
                    for half in range(2):
                        wait_full(act, step, half)
                        if i and half == 0:
                            wait_full(act, ("router", i - 1))
                        copy(hf[:, 4 * half:4 * half + 4, :], pb(step, half)[:, :].rearrange("p (a b) -> p a b", a=4))\
                            .then_inc(is_free(step, half), 1)
                elif kind in ("hT", "mixT"):
                    k = plan.ht_no[step]
                    c = ht_cols(step)
                    if k >= TPS:
                        prev = plan.ht_last(plan.ht[k - TPS])
                        wait_full(act, prev, bank_uses(prev) - 1)
                    for half in range(2):
                        if kind == "hT":
                            wait_full(act, step, half)
                            src = pb(step, half)[:, :]
                        else:
                            wait_raw(act, step)
                            src = raw_of(step)[:, half * 512:half * 512 + 512]
                        copy(hTh[:, 4 * half:4 * half + 4, c], src.rearrange("p (a b) -> p a b", a=4))\
                            .then_inc(high, 1)
                elif kind == "hn1":
                    k = head_norms.index(step)
                    wait_full(act, step)
                    if k:
                        act.wait_ge(hsum, k)
                    if before("z", step):
                        act.wait_ge(zg_done, before("z", step))
                    act.activation(sqb[:, :], pb(step)[:, :], ACT.Square).then_inc(hsq, 1)
                elif kind == "vc":
                    s, m = step[1], step[2]
                    wait_full(act, step)
                    prev = ("vt", s, 0) if m else ("hn3", "qk", s * TPS + TPS - 1)
                    wait_full(act, prev)
                    copy(qn[:, :].rearrange("p (b r c) -> p b r c", b=TPS, r=ROWS),
                         pb(step)[:, :].rearrange("p (r b c) -> p b r c", b=TPS, r=ROWS)).then_inc(is_free(step), 1)
                elif kind == "dtp":
                    wait_full(act, step)
                    if step[1]:
                        act.wait_ge(conv_out, 1 + nth("conv", step[1] - 1, 3))
                    copy(cth[0:16, :], pb(step)[0:16, :]).then_inc(is_free(step), 1)
                elif kind == "dtt":
                    wait_full(act, step)
                    if step[1]:
                        act.wait_ge(dt_v, 4 * step[1])
                    copy(dtr[:, :, :].rearrange("p c h -> p (c h)"), pb(step)[:, 0:64]).then_inc(is_free(step), 1)
                elif kind == "vt":
                    s, m = step[1], step[2]
                    wait_full(act, step)
                    if s:
                        wait_full(act, ("nav", s - 1, 3))
                    copy(v_sb[:, :, m * P:(m + 1) * P], pb(step)[:, :].rearrange("p (b d) -> p b d", b=TPS))\
                        .then_inc(is_free(step), 1)
                elif kind == "mv":
                    wait_full(act, step)
                    wait_na_pool(act)
                    copy(xv[:, step[2], :], pb(step)[:, :]).then_inc(is_free(step), 1)
                elif kind == "conv":
                    k = nth(*step)
                    act.wait_ge(conv_sum, k + 1)
                    if k:
                        act.wait_ge(conv_out, k)
                    act.activation(cth[:, :], cacc[:, k % 2, :], ACT.Tanh).then_inc(conv_th, 1)
                elif kind == "convT":
                    s, m = step[1], step[2]
                    if m <= 4:
                        wait_full(act, step)
                        src = pb(step)[:, :].rearrange("p (a b) -> p a b", a=TPS)
                        if s:
                            act.wait_ge(xdt_done, TPS * s)
                            act.wait_ge(xw_done, 6 * s)
                            wait_full(act, ("sy", s - 1, TPS - 2), 3)
                            act.wait_ge(y_done, TPS * s)
                        dst = xs[:, :, m * P:(m + 1) * P] if m < 4 else btm[:, :, :]
                        copy(dst, src).then_inc(is_free(step), 1)
                elif kind == "u":
                    wait_full(act, step)
                    k = nth(*step)
                    if k:
                        wait_full(act, ("uT",) + uses_u[k - 1], 1)
                    else:
                        act.wait_ge(init_p, 2)
                    copy(up[:, 8:T + 8], pb(step)[:, :]).then_inc(is_free(step), 1)
                elif kind == "z":
                    k = nth(*step)
                    wait_full(act, step)
                    if k:
                        act.wait_ge(zg_done, k)
                    act.wait_ge(hsum, before("hn1", step))
                    act.activation(sqb[:, :], pb(step)[:, :], ACT.Tanh, scale=0.5).then_inc(zt_done, 1)
                elif kind == "dtv":
                    k = nth(*step)
                    act.wait_ge(dt_v, 4 * k + 1)
                    link(act.activation(dts[:, :, :], dt2[:, :, :], ACT.Exp, scale=-1.0))
                    act.activation(dts[:, :, :], dts[:, :, :], ACT.Ln, bias=1.0).then_inc(dt_a, 1)
                elif kind == "dt":
                    k = nth(*step)
                    act.wait_ge(dt_v, 4 * k + 3)
                    act.activation(ecs[:, :, :, :], cs[:, :, :, :], ACT.Exp)
                    act.activation(edec[:, :, :], tot[:, :, :], ACT.Exp)
                    act.activation(wst[:, :, :, :], wst[:, :, :, :], ACT.Exp).then_inc(dt_a, 1)
                elif kind == "sdec":
                    s, c = step[1], step[2]
                    for dr in range(2):
                        for hh in range(2):
                            wait_released(act, step, 2 + 2 * dr + hh)
                            for h in range(4 * hh, 4 * hh + 4):
                                last = act.activation(dec[:, dr, h, :], dec[:, dr, h, :], ACT.Exp,
                                                      bias=ncs[:, dr, c, h:h + 1])
                            last.then_inc(e_done, 1)
                elif kind == "sy":
                    k = nth(*step)
                    act.wait_ge(y_done, k + 1)
                    for g in range(SSD_G):
                        r = slice(g * 256, g * 256 + 256)
                        last = act.activation(y2[:, r], y1[:, r], ACT.Square, accum_out=yss[:, g:g + 1])
                    last.then_inc(ysq_done, 1)
                elif kind in ("na1", "xs1"):
                    k = softmaxes.index(step)
                    act.wait_ge(max_done, k + 1)
                    w = 256 if kind == "xs1" or step[2] < 3 else P
                    if kind == "xs1":
                        wait_transposed(act, k)
                    for j in range(4):
                        src = pb(step, j // 2)[:, (j % 2) * 256:(j % 2) * 256 + 256] if kind == "xs1" else prob[:, j, 0:w]
                        ins = act.activation(prob[:, j, 0:w], src, ACT.Exp, bias=nmx[:, j:j + 1],
                                             accum_out=psm[:, j:j + 1])
                        if kind == "xs1" and j % 2:
                            ins.then_inc(is_free(step, j // 2), 1)
                    if kind == "na1":
                        ins.then_inc(exp_done, 1)
                elif kind in ("na2", "xs2"):
                    wait_full(act, step, 0)
                    copy(probT[:, 0:4, :], pb(step, 0)[:, :].rearrange("p (a b) -> p a b", a=4))\
                        .then_inc(is_free(step, 0), 1)
                elif kind == "xav":
                    wait_full(act, step)
                    if step[1]:
                        wait_full(act, ("xo", step[1] - 1), 1)
                    copy(oTh[:, :], pb(step)[:, :]).then_inc(o_high, 1)

            act.wait_ge(r_v, 1)
            act.activation(r_g2[:, :, :], r_g[:, :, :], ACT.Exp).then_inc(r_a, 1)
            act.wait_ge(r_v, 2)
            act.activation(r_t[:, 1, :], r_t[:, 0, :], ACT.Exp).then_inc(r_a, 1)

            def rows_high(n, i):
                if not isinstance(n, int) or n > 1:
                    act.wait_ge(gu_full, n - 1)
                for half in range(2):
                    act.wait_ge(xg_full, 2 * n + half + 1)
                    copy(xgH[i][:, 4 * half:4 * half + 4, :],
                         bank[B_XG[half]][:, :].rearrange("p (a b) -> p a b", a=4)).then_inc(xg_high, 1)

            def weights_high(n, i, js):
                for j in js:
                    act.wait_ge(eraw_full[j], 16 * (n + 1))
                    if not isinstance(n, int) or n > 1:
                        act.wait_ge(*((gu_full, n - 1) if j < GU_PIECES else (y_full, 2 * n - 2)))
                    copy(ew_parts(i)[j][0], as_piece(eraw[j], j)).then_inc(ew_high, 1)

            def hidden_tanh(n, i):
                act.wait_ge(gu_full, n + 1)
                if not isinstance(n, int) or n > 0:
                    act.wait_ge(hb_done, n)
                act.activation(eth[:, :], bank[B_GU[i]][:, 0:DE], ACT.Tanh, scale=0.5).then_inc(th_done, 1)

            def hidden_high(n):
                act.wait_ge(hb_full, n + 1)
                if not isinstance(n, int) or n > 0:
                    act.wait_ge(y_full, 2 * n)
                copy(hbH[:, :, :], bank[B_HB][:, 0:2 * P].rearrange("p (a b) -> p a b", a=2)).then_inc(hb_high, 1)

            def y_out(n, i, stores):
                act.wait_ge(y_full, 2 * n + 1)
                if not (isinstance(stores, int) and stores == 0):
                    act.wait_ge(ey_st[i], 16 * stores)
                copy(ey[i][:, 0:512], bank[B_Y[0]][:, :]).then_inc(y_lo, 1)

            gu, dn = range(GU_PIECES), range(GU_PIECES, PIECES)
            weights_high(0, 0, range(PIECES))
            weights_high(1, 1, range(PIECES))
            rows_high(0, 0)
            rows_high(1, 1)
            hidden_tanh(0, 0)

            def step(n, i, it):
                last = isinstance(n, int) and n == NE - 1
                hidden_high(n - 1)
                if not last:
                    rows_high(n + 1, 1 - i)
                    weights_high(n + 1, 1 - i, gu)
                hidden_tanh(n, i)
                y_out(n - 1, 1 - i, it)
                if not last:
                    weights_high(n + 1, 1 - i, dn)

            pipeline(act, step)
            hidden_high(NE - 1)
            y_out(NE - 1, 1, NE // 2 - 1)

            def more(b):
                n = b + NE
                rows_high(n, 0)
                weights_high(n, 0, range(PIECES))
                hidden_tanh(n, 0)
                hidden_high(n)
                y_out(n, 0, b + NE // 2)

            further(act, more)

        @block.vector
        def _(dve):
            chain = [0]

            def link(ins):
                chain[0] += 1
                ins.then_inc(s_chain, 1)
                dve.wait_ge(s_chain, chain[0])

            tt, ts, stt = dve.tensor_tensor, dve.tensor_scalar, dve.scalar_tensor_tensor
            dve.wait_ge(first_ld, 16 * N_FIRST)

            def derive_constants():
                dve.wait_ge(const_ld, 16 * N_CONST)
                dve.tensor_copy(tri_r[:, :, :], tri_in).then_inc(init, 1)
                ts(ones_r[:, :], ident[:, :], 0.0, 1.0, ALU.mult, ALU.add).then_inc(init, 1)
                ts(g_na[:, 0:1], g_na[:, 0:1], NA_D ** -0.5, None, ALU.mult).then_inc(init, 1)
                ts(g_xa[:, 0:1], g_xa[:, 0:1], XA_D ** -0.5, None, ALU.mult).then_inc(init, 1)
                ts(cwh[:, :, :], cw[:, :, :], 0.5, None, ALU.mult).then_inc(init, 1)
                ts(cbh[:, :], cb[:, :], 0.5, None, ALU.mult).then_inc(init, 1)
                tt(bias_in[:, :, :, :, :].rearrange("p a b r c -> p (a b r) c"),
                   bias_in[:, :, :, :, :].rearrange("p a b r c -> p (a b r) c"),
                   mask.unsqueeze(1).to_broadcast([P, 4 * ROWS, 32]), ALU.add).then_inc(init, 1)
                dve.wait_ge(init_a, 1)
                ts(a_row[:, :], a_row[:, :], -1.0, None, ALU.mult).then_inc(init, 1)
                dve.wait_ge(init, N_INIT)
                dve.wait_ge(init_p, 2)

            def per_head(v, n):
                return v.unsqueeze(2).to_broadcast([v.shape[0], v.shape[1], n])

            def heads(v, h):
                return v.rearrange("p (h d) -> p h d", h=h)

            def normalise(step):
                w = 256 if step[0] == "xs1" or step[2] < 3 else P
                if step[0] == "xs1":
                    wait_released(dve, step, 1)
                else:
                    dve.wait_ge(exp_done, 1 + nth(*step))
                link(dve.reciprocal(prs[:, :], psm[:, :]))
                tt(prob[:, :, 0:w], prob[:, :, 0:w], per_head(prs[:, :], w), ALU.mult).then_inc(prob_done, 1)

            for step in TL:
                kind = step[0]
                if kind == "init":
                    derive_constants()
                elif kind == "w":
                    u, q = step[1], step[2]
                    dve.wait_ge(w_high, 1 + nth(*step))
                    wh, wl = unit_w(u)
                    cols = slice(q * 1024, (q + 1) * 1024)
                    src, h, lo = raw_of(step)[:, :], wh[:, cols].bitcast(F32), wl[:, cols]
                    if u < 10 and u % 5 == U_V:
                        src, h, lo = (x.rearrange("p (k n) -> p k n", k=2)[:, :, 0:272] for x in (src, h, lo))
                    tt(lo, src, h, ALU.subtract).then_inc(w_low, 1)
                elif kind == "norm":
                    st, i = step[1], step[2]
                    k = nth(*step)
                    dve.wait_ge(rs_done, k + 1)
                    if st != "mix":
                        dve.wait_ge(gain_ld[st], 16)
                    src = raw_of(step)[:, :] if st in ("mix", "mem") else x_sb[:, i, :]
                    to, g = NORMED[st]
                    stt(to[:, :], src, rs[:, k:k + 1], g[:, :], ALU.mult, ALU.mult).then_inc(xn_done, 1)
                elif kind == "mixT" or kind == "hT" and step[1] != "ffn":
                    k = plan.ht_no[step]
                    c = ht_cols(step)
                    for half in range(2):
                        dve.wait_ge(high, 2 * k + half + 1)
                        src = pb(step, half)[:, :] if kind == "hT" else raw_of(step)[:, half * 512:half * 512 + 512]
                        f = slice(4 * half, 4 * half + 4)
                        tt(hTl[:, f, c], src.rearrange("p (a b) -> p a b", a=4), hTh[:, f, c].bitcast(F32),
                           ALU.subtract).then_inc(low, 1)
                elif kind == "hn1":
                    k = nth(*step)
                    g, n = HN_GROUPS[step[1]]
                    dve.wait_ge(hsq, k + 1)
                    if k:
                        dve.wait_ge(hrms, k)
                    dve.tensor_reduce(hss[:, 0:g], heads(sqb[:, :], g), AX_X, ALU.add).then_inc(hsum, 1)
                elif kind == "hn2":
                    k = nth(*step)
                    g, n = HN_GROUPS[step[1]]
                    first = ("hn1",) + step[1:]
                    dve.wait_ge(hrms, k + 1)
                    if k:
                        wait_full(dve, ("hn3",) + head_norms[k - 1][1:])
                    if before("vt", step):
                        wait_full(dve, ("vt", before("vt", step) // 2 - 1, 1))
                    tt(heads(qn[:, :], g), heads(pb(first)[:, :], g), per_head(hrs[:, k % 2, 0:g], n), ALU.mult)\
                        .then_inc(hnorm, 1)
                elif kind == "hn3":
                    st, i = step[1], step[2]
                    wait_full(dve, step)
                    b = pb(step)
                    c = slice((i % TPS) * P, (i % TPS + 1) * P)
                    if st == "qk":
                        for pair in range(2):
                            q = b[:, pair * P:(pair + 1) * P].rearrange("p (r c) -> p r c", r=2)
                            r0 = 2 * (i % TPS)
                            ts(qT[:, pair, 0:384].rearrange("p (m r c) -> p r m c", m=3, r=ROWS)[:, r0:r0 + 2, :, :],
                               q[:, :, 8:56].rearrange("p r (m c) -> p r m c", m=3), g_na[:, 0:1], None, ALU.mult)
                            for side in range(2):
                                at = 384 + 64 * side + 8 * r0
                                ts(qT[:, pair, at:at + 16].rearrange("p (r c) -> p r c", r=2),
                                   q[:, :, 56 * side:56 * side + 8], g_na[:, 0:1], None, ALU.mult)
                        ts(kT[:, :, c], b[:, 256:512].rearrange("p (a t) -> p a t", a=2), g_na[:, 1:2], None,
                           ALU.mult).then_inc(is_free(step), 1)
                    elif st == "mk":
                        wait_na_pool(dve)
                        ts(xkT[:, :, c], b[:, :].rearrange("p (a t) -> p a t", a=4), g_xa[:, 1:2], None, ALU.mult)\
                            .then_inc(is_free(step), 1)
                    else:
                        ts(xqT[:, :, :], b[:, :].rearrange("p (a t) -> p a t", a=4), g_xa[:, 0:1], None, ALU.mult)\
                            .then_inc(is_free(step), 1)
                elif kind == "conv":
                    s, m = step[1], step[2]
                    k = nth(*step)
                    wait_full(dve, step)
                    b = pb(step)
                    acc = cacc[:, k % 2, :]
                    if k >= 2 and conv_steps[k - 2][2] <= 4:
                        wait_full(dve, ("convT",) + conv_steps[k - 2][1:])
                    link(ts(acc, b[:, :], cwh[:, m, 1:2], cbh[:, m:m + 1], ALU.mult, ALU.add))
                    for j, sh in ((0, -1), (2, 1), (3, 2)):
                        to = slice(max(0, -sh), T - max(0, sh))
                        frm = slice(max(0, sh), T - max(0, -sh))
                        ins = stt(acc[:, to], b[:, frm], cwh[:, m, j:j + 1], acc[:, to], ALU.mult, ALU.add)
                        if j < CONV_W - 1:
                            link(ins)
                    ins.then_inc(conv_sum, 1)
                    dve.wait_ge(conv_th, k + 1)
                    dst = cacc[:, k % 2, :] if m < 4 else (bT if m == 4 else cT)[:, :]
                    stt(dst, cth[:, :], 1.0, cacc[:, k % 2, :], ALU.add, ALU.mult).then_inc(conv_out, 1)
                elif kind == "z":
                    k = nth(*step)
                    dve.wait_ge(zt_done, k + 1)
                    if k:
                        dve.wait_ge(z_st[k - 1], 16)
                    stt(zg[:, :], sqb[:, :], 1.0, pb(step)[:, :], ALU.add, ALU.mult).then_inc(zg_done, 1)
                elif kind == "uT":
                    s, m = step[1], step[2]
                    for j in range(2):
                        r = slice(64 * j, 64 * j + 64)
                        wait_full(dve, step, j)
                        ts(wa[r, 0:T], pb(step, j)[r, :], p_scale[r, m:m + 1], None, ALU.mult)\
                            .then_inc(is_free(step, j), 1)
                elif kind == "dtv":
                    k = nth(*step)
                    s = step[1]
                    wait_released(dve, ("dtt", s))
                    by_tile = lambda v: v[:, :].unsqueeze(1).to_broadcast([P, TPS, 16])
                    link(tt(dt1[:, :, :], dtr[:, :, :], by_tile(dt_bias), ALU.add))
                    stt(dt2[:, :, :], dt1[:, :, :], -1.0, dt1[:, :, :], ALU.mult, ALU.max).then_inc(dt_v, 1)
                    dve.wait_ge(dt_a, 2 * k + 1)
                    link(stt(dts[:, :, :], dt1[:, :, :], 0.0, dts[:, :, :], ALU.max, ALU.add))
                    link(tt(la[:, :, :], dts[:, :, :], by_tile(a_row), ALU.mult))
                    link(dve.tensor_copy(laH[:, :, :], la[:, :, :]))
                    tt(laL[:, :, :], la[:, :, :], laH[:, :, :].bitcast(F32), ALU.subtract).then_inc(dt_v, 1)
                elif kind == "dt":
                    k = nth(*step)
                    wait_full(dve, step)
                    b = pb(step)
                    link(dve.tensor_copy(cs[:, :, :, :].rearrange("p d c h -> p (d c h)"), b[:, 0:64]))
                    dve.tensor_copy(tot[:, :, :].rearrange("p c h -> p (c h)"), b[:, 64:128])\
                        .then_inc(is_free(step), 1)
                    wait_released(dve, step)
                    ts(ncs[:, :, :, :], cs[:, :, :, :], -1.0, None, ALU.mult)
                    for dr in range(2):
                        ins = tt(wst[:, dr, :, :], tot[:, :, dr * 8:dr * 8 + 8], cs[:, dr, :, :], ALU.subtract)
                    ins.then_inc(dt_v, 1)
                    dve.wait_ge(dt_a, 2 * k + 2)
                    for dr in range(2):
                        ins = tt(wst[:, dr, :, :], wst[:, dr, :, :], dts[:, :, dr * 8:dr * 8 + 8], ALU.mult)
                    ins.then_inc(dt_v, 1)
                elif kind in ("sback", "sy"):
                    s, c = step[1], step[2]
                    if kind == "sy":
                        k = nth(*step)
                        if k:
                            wait_full(dve, ("sout",) + chunks[k - 1])
                            dve.wait_ge(ssd_st[(k - 1) // TPS], 16 * ((k - 1) % TPS + 1))
                        for g in range(SSD_G):
                            wait_full(dve, step, 1 + g)
                            b, r, hd = pb(step, 1 + g), slice(256 * g, 256 * g + 256), slice(4 * g, 4 * g + 4)
                            ins = tt(heads(y1[:, r], 4), heads(b[:, 0:256], 4), per_head(ecs[:, 0, c, hd], SSD_P),
                                     ALU.mult)
                            if c < TPS - 1:
                                ins = tt(heads(y2[:, r], 4), heads(b[:, 256:512], 4),
                                         per_head(ecs[:, 1, c, hd], SSD_P), ALU.mult)
                            ins.then_inc(is_free(step, 1 + g), 1)
                        wait_released(dve, step, 1)
                        wait_released(dve, step, 2)
                        if c < TPS - 1:
                            link(tt(y1[:, :], y1[:, :], y2[:, :], ALU.add))
                        link(tt(heads(y2[:, :], 8), heads(xs[:, c, :], 8), per_head(d_row[:, :], SSD_P), ALU.mult))
                        link(tt(y1[:, :], y1[:, :], y2[:, :], ALU.add))
                    j = 3 if kind == "sy" else 0
                    first = kind == "sback" and c == TPS - 1
                    old = S_f[:, :] if kind == "sy" else None if first else S_b[:, c, :]
                    new = S_f[:, :] if kind == "sy" else S_b[:, c - 1, :]
                    dr = 0 if kind == "sy" else 1
                    blocks = [(g, slice(64 * g, 64 * g + 64), slice(256 * g, 256 * g + 256)) for g in range(SSD_G)]
                    if kind == "sback" or c < TPS - 1:
                        wait_full(dve, step, j)
                        for g, r, cols in blocks if not first else ():
                            link(tt(heads(new[r, :], 4), heads(old[r, :], 4),
                                    per_head(edec[r, c, dr * 8 + 4 * g:dr * 8 + 4 * g + 4], SSD_P), ALU.mult))
                        for g, r, cols in blocks:
                            if first:
                                ins = dve.tensor_copy(new[r, :], pb(step, j)[r, cols])
                            else:
                                ins = tt(new[r, :], new[r, :], pb(step, j)[r, cols], ALU.add)
                        ins.then_inc(is_free(step, j), 1)
                        wait_released(dve, step, j)
                    if kind == "sy":
                        wait_full(dve, step, 0)
                        tt(y1[:, :], y1[:, :], pb(step, 0)[:, :], ALU.add).then_inc(is_free(step, 0), 1)
                        wait_released(dve, step, 0)
                        dve.wait_ge(z_ld, 16 * (k + 1))
                        tt(y1[:, :], y1[:, :], zg[:, :], ALU.mult).then_inc(y_done, 1)
                        dve.wait_ge(yrs_done, k + 1)
                        for g in range(SSD_G):
                            r = slice(256 * g, 256 * g + 256)
                            ins = ts(y2[:, r], y1[:, r], yrs[:, g:g + 1], None, ALU.mult)
                        ins.then_inc(yn_done, 1)
                elif kind == "sdec":
                    s, c = step[1], step[2]
                    k = nth(*step)
                    if c == 0:
                        dve.memset(S_f[:, :], 0.0).then_inc(sf_done, 1)
                        dve.wait_ge(sf_done, s + 1)
                    for g in range(SSD_G):
                        wait_full(dve, step, g)
                        for dr in range(2):
                            ins = tt(cbm[:, dr, g, :], pb(step, g)[:, 0:P], tri[:, dr, :], ALU.mult)
                        ins.then_inc(is_free(step, g), 1)
                    if k:
                        wait_full(dve, ("sy",) + chunks[k - 1], 0)
                    for dr in range(2):
                        for g in range(SSD_G):
                            j = 2 + 2 * dr + g
                            wait_full(dve, step, j)
                            tt(dec[:, dr, 4 * g:4 * g + 4, :], pb(step, j)[:, :].rearrange("p (h l) -> p h l", h=4),
                               per_head(cs[:, dr, c, 4 * g:4 * g + 4], P), ALU.min).then_inc(is_free(step, j), 1)
                    for g in range(SSD_G):
                        wait_released(dve, step, g)
                    for dr in range(2):
                        for g in range(SSD_G):
                            dve.wait_ge(e_done, 4 * k + 2 * dr + g + 1)
                            d = dec[:, dr, 4 * g:4 * g + 4, :]
                            ins = tt(d, d, cbm[:, dr, g, :].unsqueeze(1).to_broadcast([P, 4, P]), ALU.mult)
                    ins.then_inc(t_done, 1)
                elif kind == "sout":
                    k = nth(*step)
                    wait_full(dve, step)
                    dve.wait_ge(yn_done, k + 1)
                    for j in range(4):
                        ins = ts(y1[:, j * P:(j + 1) * P], pb(step)[:, j * P:(j + 1) * P], ssd_g[:, j:j + 1], None, ALU.mult)
                    ins.then_inc(is_free(step), 1)
                elif kind == "na1":
                    s, m = step[1], step[2]
                    k = softmaxes.index(step)
                    w = 256 if m < 3 else P
                    wait_transposed(dve, k)
                    for par in range(2):
                        wait_full(dve, step, par)
                        for pair in range(2):
                            dst = prob[:, 2 * par + pair, 0:w]
                            src = pb(step, par)[:, pair * w:(pair + 1) * w]
                            if m < 3:
                                dst, src = (x.rearrange("p (b r c) -> p b r c", b=2, r=ROWS) for x in (dst, src))
                                bias = bias_in[:, par, pair, :, :].rearrange("p r (b c) -> p b r c", b=2)
                            else:
                                bias = bias_ed[:, par, pair, :, :].rearrange("p r c -> p (r c)")
                            ins = tt(dst, src, bias, ALU.add)
                        ins.then_inc(is_free(step, par), 1)
                    for par in range(2):
                        wait_released(dve, step, par)
                    link(dve.tensor_reduce(mx[:, :], prob[:, :, 0:w], AX_X, ALU.max))
                    ts(nmx[:, :], mx[:, :], -1.0, None, ALU.mult).then_inc(max_done, 1)
                    normalise(step)
                elif kind == "xs1":
                    for half in range(2):
                        wait_full(dve, step, half)
                        ins = dve.tensor_reduce(mx[:, 2 * half:2 * half + 2],
                                                pb(step, half)[:, :].rearrange("p (a c) -> p a c", a=2), AX_X, ALU.max)
                        link(ins)
                    ts(nmx[:, :], mx[:, :], -1.0, None, ALU.mult).then_inc(max_done, 1)
                    normalise(step)
                elif kind in ("na2", "xs2"):
                    n_bk = prob_banks(step)
                    if n_bk == 2:
                        wait_full(dve, step, 1)
                        dve.tensor_copy(probT[:, 4:8, :], pb(step, 1)[:, :].rearrange("p (a b) -> p a b", a=4))\
                            .then_inc(is_free(step, 1), 1)
                elif kind == "nav":
                    s, m = step[1], step[2]
                    wait_full(dve, step)
                    if s and m == 0:
                        dve.wait_ge(nao_st[s - 1], 32)
                    b = pb(step)
                    to = nao[:, :, :].rearrange("p a (r c) -> p a r c", r=ROWS)
                    if m < 3:
                        dve.tensor_copy(to[:, :, :, 8 + 16 * m:24 + 16 * m],
                                        b[:, 0:256].rearrange("p (a r c) -> p a r c", a=2, r=ROWS))\
                            .then_inc(is_free(step), 1)
                    else:
                        frm = b[:, 0:256].rearrange("p (a e r c) -> p a e r c", a=2, e=2, r=ROWS)
                        for side in range(2):
                            ins = dve.tensor_copy(to[:, :, :, 56 * side:56 * side + 8], frm[:, :, side, :, :])
                        ins.then_inc(is_free(step), 1)
                elif kind == "xav":
                    dve.wait_ge(o_high, step[1] + 1)
                    tt(oTl[:, :], pb(step)[:, :], oTh[:, :].bitcast(F32), ALU.subtract).then_inc(o_low, 1)
                elif kind == "out":
                    i, half = step[2:]
                    wait_full(dve, step)
                    dve.wait_ge(x_ld[i // TPS], 16 * TPS)
                    r = slice(512 * half, 512 * half + 512)
                    tt(x_sb[:, i, r], x_sb[:, i, r], pb(step)[:, :], ALU.add).then_inc(x1, 1)
                elif kind == "xo":
                    i = step[1]
                    for half in range(2):
                        wait_full(dve, step, half)
                        r = slice(512 * half, 512 * half + 512)
                        tt(x_sb[:, i, r], x_sb[:, i, r], pb(step, half)[:, :], ALU.add).then_inc(x2, 1)
                elif kind == "router":
                    i = step[1]
                    dve.wait_ge(router_ld, 64)
                    wait_full(dve, step)
                    tt(logits[:, i, :], pb(step)[:, 0:NG + NE], router_b[:, :], ALU.add).then_inc(is_free(step), 1)

            def over(v, n):
                return v.unsqueeze(2).to_broadcast([P, v.shape[1], n])

            def along(v, n):
                return v.unsqueeze(1).to_broadcast([P, n, v.shape[1]])

            wait_released(dve, ("router", NT - 1))
            dve.wait_ge(r_pool, 3)
            dve.wait_ge(hn_st, 16 * NT)
            gl = logits[:, :, 0:NG]
            link(dve.tensor_reduce(r_max[:, 0, :], gl, AX_X, ALU.max))
            tt(r_g[:, :, :], gl, over(r_max[:, 0, :], NG), ALU.subtract).then_inc(r_v, 1)

            def first_of_max(vals, m, idx, eq, n):
                link(tt(eq, vals, over(m, n), ALU.is_ge))
                link(stt(eq, eq, -64.0, along(iota_e[:, 0:n], NT), ALU.mult, ALU.add))
                link(dve.tensor_reduce(idx, eq, AX_X, ALU.min))
                link(ts(idx, idx, 64.0, None, ALU.add))

            eqg = r_eq[:, :, 0:NG]
            first_of_max(gl, r_max[:, 0, :], r_idx[:, 0, :], eqg, NG)
            link(tt(eqg, along(iota_e[:, 0:NG], NT), over(r_idx[:, 0, :], NG), ALU.is_equal))
            link(ts(eqg, eqg, 1.0, 1e30, ALU.subtract, ALU.mult))
            link(tt(r_e[:, :, :].rearrange("p t (g e) -> p t g e", g=NG),
                    logits[:, :, NG:].rearrange("p t (g e) -> p t g e", g=NG),
                    eqg.unsqueeze(3).to_broadcast([P, NT, NG, EPG]), ALU.add))
            for c in range(2):
                m, idx = r_max[:, 1 + c, :], r_idx[:, 1 + c, :]
                link(dve.tensor_reduce(m, r_e[:, :, :], AX_X, ALU.max))
                first_of_max(r_e[:, :, :], m, idx, r_eq[:, :, :], NE)
                link(tt(oh[:, c, :, :], along(iota_e[:, 0:NE], NT), over(idx, NE), ALU.is_equal))
                if c == 0:
                    link(stt(r_e[:, :, :], oh[:, 0, :, :], -2e30, r_e[:, :, :], ALU.mult, ALU.add))
            tt(r_t[:, 0, :], r_max[:, 2, :], r_max[:, 1, :], ALU.subtract).then_inc(r_v, 1)
            link(tt(cnt_b[:, :, :], oh[:, 0, :, :], oh[:, 1, :, :], ALU.add))
            link(ts(tri_b[:, :], iota_p[:, :], token0[:, 0:1], None, ALU.is_gt))
            ts(ones_b[:, :], iota_p[:, :], 0.0, 1.0, ALU.mult, ALU.add).then_inc(r_v, 1)
            dve.wait_ge(r_a, 2)
            link(dve.tensor_reduce(r_t[:, 2, :], r_g2[:, :, :], AX_X, ALU.add))
            link(ts(r_t[:, 3, :], r_t[:, 1, :], 1.0, None, ALU.add))
            link(tt(r_t[:, 2, :], r_t[:, 2, :], r_t[:, 3, :], ALU.mult))
            link(dve.reciprocal(r_t[:, 3, :], r_t[:, 2, :]))
            link(ts(gates[:, 0, :], r_t[:, 3, :], 0.5, None, ALU.mult))
            link(tt(gates[:, 1, :], gates[:, 0, :], r_t[:, 1, :], ALU.mult))
            dve.wait_ge(r_pe, 1)
            b = bank[B_R]
            link(dve.tensor_copy(rank[:, :, :].rearrange("p a b -> p (a b)"), b[:, 0:NT * NE]))
            link(dve.tensor_copy(n_e[:, :], b[:, NT * NE:NT * NE + NE]))
            def whole_blocks(dst, src):
                link(ts(dst, src, 1.0 / P, 0.5 / P - 0.5, ALU.mult, ALU.add))
                link(ts(dst, dst, ROUND, None, ALU.add))
                link(ts(dst, dst, ROUND, 0.0, ALU.subtract, ALU.max))

            dve.memset(ov[:, 2, :], 1.0)
            link(ts(n_e[:, :], n_e[:, :], 1.0, None, ALU.subtract))
            whole_blocks(ov[:, 0, :], n_e[:, :])
            link(dve.tensor_tensor_scan(ov[:, 1, :], ov[:, 2, :], ov[:, 0, :], 0.0, ALU.mult, ALU.add))
            link(tt(ov[:, 3, :], ov[:, 1, :], ov[:, 0, :], ALU.subtract))
            for table, place in ((rank[:, :, :].unsqueeze(1), 0), (ov[:, 3, :].unsqueeze(1).unsqueeze(1), 1)):
                link(tt(r_both, oh[:, :, :, :], table.to_broadcast([P, 2, NT, NE]), ALU.mult))
                link(dve.tensor_reduce(pos[:, place, :, :], r_both, AX_X, ALU.add))
            whole_blocks(pos[:, 2, :, :], pos[:, 0, :, :])
            link(stt(pos[:, 5, :, :], pos[:, 2, :, :], -float(P), pos[:, 0, :, :], ALU.mult, ALU.add))
            link(tt(pos[:, 1, :, :], pos[:, 1, :, :], pos[:, 2, :, :], ALU.add))
            link(stt(pos[:, 1, :, :], pos[:, 1, :, :], float(NE - 1), r_idx[:, 1:3, :], ALU.add, ALU.subtract))
            link(stt(pos[:, 3, :, :], pos[:, 2, :, :], 1.0, pos[:, 1, :, :], ALU.min, ALU.mult))
            link(tt(pos[:, 4, :, :], pos[:, 3, :, :], r_idx[:, 1:3, :], ALU.add))
            link(stt(pos[:, 1, :, :], pos[:, 4, :, :], float(P), pos[:, 5, :, :], ALU.mult, ALU.add))
            link(dve.tensor_copy(slot[:, :, :], pos[:, 1, :, :]))
            link(ts(pos[:, 3, :, :], pos[:, 1, :, :], float(NE * P), 4.0 * NE * P, ALU.is_lt, ALU.mult))
            link(stt(slot_o[:, :, :], pos[:, 1, :, :], -float(NE * P), pos[:, 3, :, :], ALU.add, ALU.add))
            flat = lambda v: v.rearrange("p c t -> p (c t)")
            tt(oneh_p[:, :, :], along(iota_p[:, :], 2 * NT), over(flat(pos[:, 5, :, :]), P), ALU.is_equal)
            link(tt(oneh_b[:, :, :], along(iota_e[:, :], 2 * NT), over(flat(pos[:, 4, :, :]), NB + 1), ALU.is_equal))
            for c in range(2):
                o = oneh_b[:, c * NT:(c + 1) * NT, :]
                ins = tt(o, o, over(token1[:, :], NB + 1), ALU.mult)
            ins.then_inc(r_v, 1)
            dve.wait_ge(r_pe, 2)
            b = bank[B_HB]
            link(ts(idt[:, :], b[:, 0:NB + 1], 0.0, 5000.0, ALU.is_equal, ALU.mult))
            stt(ids[:, :], b[:, 0:NB + 1], -1.0, idt[:, :], ALU.add, ALU.add).then_inc(r_v, 1)
            dve.wait_ge(r_v, R_STAGES)

            def further_experts():
                link(tt(ov3[:, 0, :, :], over(iota_e[:, 0:NO], NE), along(ov[:, 3, :], NO), ALU.is_ge))
                link(tt(ov3[:, 1, :, :], over(iota_e[:, 0:NO], NE), along(ov[:, 1, :], NO), ALU.is_lt))
                link(tt(ov3[:, 0, :, :], ov3[:, 0, :, :], ov3[:, 1, :, :], ALU.mult))
                link(tt(ov3[:, 0, :, :], ov3[:, 0, :, :], along(iota_e[:, 0:NE], NO), ALU.mult))
                link(dve.tensor_reduce(ovx[:, :], ov3[:, 0, :, :], AX_X, ALU.add))
                link(dve.tensor_copy(ovi[:, 0:NO], ovx[:, :]))
                dve.tensor_copy(ovi[:, NO:NO + 1], ov[:, 1, NE - 1:NE]).then_inc(r_v, 1)

            def row_numbers(n, i, loads):
                if not (isinstance(loads, int) and loads == 0):
                    dve.wait_ge(xg_ld[i], 16 * loads)
                col = ids[:, n:n + 1] if isinstance(n, int) else ids[:, bass.ds(n, 1)]
                dve.tensor_copy(idc[i][:, :], col).then_inc(idc_done, 1)

            def rows_low(n, i):
                for half in range(2):
                    dve.wait_ge(xg_high, 2 * n + half + 1)
                    f = slice(4 * half, 4 * half + 4)
                    tt(xgL[i][:, f, :], bank[B_XG[half]][:, :].rearrange("p (a b) -> p a b", a=4),
                       xgH[i][:, f, :].bitcast(F32), ALU.subtract).then_inc(xg_low, 1)

            def weights_low(n, i, js):
                for j in js:
                    dve.wait_ge(ew_high, PIECES * n + j + 1)
                    h, lo = ew_parts(i)[j]
                    tt(lo, as_piece(eraw[j], j), h.bitcast(F32), ALU.subtract).then_inc(ew_low, 1)

            def hidden(n, i):
                dve.wait_ge(th_done, n + 1)
                if not isinstance(n, int) or n > 0:
                    dve.wait_ge(hb_full, n)
                b = bank[B_GU[i]]
                link2(stt(ehb[:, :], eth[:, :], 1.0, b[:, 0:DE], ALU.add, ALU.mult), n)
                tt(ehb[:, :], ehb[:, :], b[:, DE:2 * DE], ALU.mult).then_inc(hb_done, 1)

            def link2(ins, n):
                ins.then_inc(hb_part, 1)
                dve.wait_ge(hb_part, n + 1)

            def hidden_low(n):
                dve.wait_ge(hb_high, n + 1)
                tt(hbL[:, :, :], bank[B_HB][:, 0:2 * P].rearrange("p (a b) -> p a b", a=2),
                   hbH[:, :, :].bitcast(F32), ALU.subtract).then_inc(hb_low, 1)

            def y_out(n, i, stores):
                dve.wait_ge(y_full, 2 * n + 2)
                if not (isinstance(stores, int) and stores == 0):
                    dve.wait_ge(ey_st[i], 16 * stores)
                dve.tensor_copy(ey[i][:, 512:1024], bank[B_Y[1]][:, :]).then_inc(y_hi, 1)

            gu, dn = range(GU_PIECES), range(GU_PIECES, PIECES)
            row_numbers(0, 0, 0)
            row_numbers(1, 1, 0)
            dve.wait_ge(ew_low, PIECES)
            weights_low(1, 1, gu)
            rows_low(0, 0)
            row_numbers(2, 0, 1)
            rows_low(1, 1)
            weights_low(1, 1, dn)
            hidden(0, 0)
            further_experts()

            def step(n, i, it):
                last = isinstance(n, int) and n == NE - 1
                if not last:
                    row_numbers(n + 2, i, it + 1)
                hidden_low(n - 1)
                if not last:
                    rows_low(n + 1, 1 - i)
                    weights_low(n + 1, 1 - i, gu)
                hidden(n, i)
                y_out(n - 1, 1 - i, it)
                if not last:
                    weights_low(n + 1, 1 - i, dn)

            pipeline(dve, step)
            hidden_low(NE - 1)
            y_out(NE - 1, 1, NE // 2 - 1)

            def more(b):
                n = b + NE
                dve.wait_ge(xg_ld[0], b * 16 + 16 * (NE // 2))
                rows_low(n, 0)
                weights_low(n, 0, range(PIECES))
                hidden(n, 0)
                hidden_low(n)
                y_out(n, 0, b + NE // 2)
                row_numbers(n + 1, 0, b + NE // 2 + 1)

            further(dve, more)

            for i in range(NT):
                for c in range(2):
                    dve.wait_ge(yg_ld[i % 2][c], 16 * (i // 2 + 1))
                    stt(x_sb[:, i, :], yg[i % 2][c][:, :], gates[:, c, i:i + 1], x_sb[:, i, :], ALU.mult, ALU.add)\
                        .then_inc(yg_used, 1)
                    dve.wait_ge(yg_used, 2 * i + c + 1)

        @block.gpsimd
        def _(pool):
            chain = [0]

            def link(ins):
                chain[0] += 1
                ins.then_inc(p_chain, 1)
                pool.wait_ge(p_chain, chain[0])

            def rsqrt(dst, tmp, src, scale, eps):
                link(pool.tensor_scalar(tmp, src, scale, eps, ALU.mult, ALU.add))
                return pool.tensor_tensor(dst, tmp, neghalf[:, 0:src.shape[1]], ALU.pow)

            def per_head(v, n):
                return v.unsqueeze(2).to_broadcast([v.shape[0], v.shape[1], n])

            def heads(v, h=SSD_H):
                return v.rearrange("p (h d) -> p h d", h=h)

            pool.memset(neghalf[:, :], -0.5)
            pool.memset(up[:, :], 0.0)
            pool.memset(wa[:, :], 0.0)
            pool.memset(wb[:, :], 0.0).then_inc(init_p, 1)
            pool.memset(S_b[:, :, :], 0.0).then_inc(init_p, 1)
            pool.wait_ge(init_p, 2)
            for step in TL:
                kind = step[0]
                if kind == "init":
                    pool.wait_ge(init, N_INIT)
                elif kind == "norm":
                    k = nth(*step)
                    pool.wait_ge(sq_done, k + 1)
                    rsqrt(rs[:, k:k + 1], ms[:, k:k + 1], ssq[:, k:k + 1], 1.0 / D, EPS).then_inc(rs_done, 1)
                elif kind == "gain":
                    name = {"mem": "norm_mem", "xa": "norm_xa", "ffn": "norm_ffn"}[step[1]]
                    pool.wait_ge(xn_done, before("norm", step))
                    if step[1] == "ffn":
                        wait_mixed(pool)
                    pool.dma_start(NORMED[step[1]][1][:, :], bass.AP(dram[name].tensor, 0, [[0, P], [1, D]])).then_inc(gain_ld[step[1]], 16)
                    if step[1] == "ffn":
                        parts = (("w_router_group", "b_router_group", 0, NG), ("w_router_expert", "b_router_expert", NG, NE))
                        for w, b_, o, m in parts:
                            pool.dma_start(router_w[:, :, o:o + m], dram[w][0].rearrange("(k p) n -> p k n", p=P))\
                                .then_inc(router_ld, 16)
                            pool.dma_start(router_b[:, o:o + m], bass.AP(dram[b_].tensor, 0, [[0, P], [1, m]]))\
                                .then_inc(router_ld, 16)
                elif kind == "hT" and step[1] == "ffn":
                    i = step[2]
                    pool.wait_ge(xn_done, 1 + nth("norm", "ffn", i))
                    pool.dma_start(hn_dram[i * P:(i + 1) * P, :], xn_ffn[:, :]).then_inc(hn_st, 16)
                elif kind == "hn1":
                    k = nth(*step)
                    g, n = HN_GROUPS[step[1]]
                    pool.wait_ge(hsum, k + 1)
                    if k >= 2:
                        pool.wait_ge(hnorm, k - 1)
                    rsqrt(hrs[:, k % 2, 0:g], hms[:, 0:g], hss[:, 0:g], 1.0 / n, EPS).then_inc(hrms, 1)
                elif kind == "z":
                    k = nth(*step)
                    pool.wait_ge(zg_done, k + 1)
                    pool.dma_start(z_dram[k], zg[:, :]).then_inc(z_st[k], 16)
                elif kind == "u":
                    s, m = step[1], step[2]
                    k = nth(*step)
                    wait_released(pool, step)
                    add = lambda o, a, b_: pool.tensor_tensor(o, a, b_, ALU.add)
                    n = T + 16
                    if k:
                        pool.wait_ge(po_st[(k - 1) // 2], 16 * ((k - 1) % 2 + 1))
                    link(add(wa[:, 1:n], up[:, 0:n - 1], up[:, 1:n]))
                    if m == 0:
                        link(add(wb[64:P, 2:n - 1], wa[64:P, 1:n - 2], wa[64:P, 3:n]))
                    else:
                        link(add(wb[:, 2:n - 1], wa[:, 1:n - 2], wa[:, 3:n]))
                        link(add(wa[:, 4:n - 3], wb[:, 2:n - 5], wb[:, 6:n - 1]))
                        link(add(wb[64:P, 8:n - 8], wa[64:P, 4:n - 12], wa[64:P, 12:n - 4]))
                    for j, w in enumerate((wa, wb)):
                        r = slice(64 * j, 64 * j + 64)
                        pool.tensor_scalar(w[r, 16:T], w[r, 16:T], p_inv[r, m, 0:1], None, ALU.mult)
                        pool.tensor_tensor(w[r, 8:16], w[r, 8:16], p_inv[r, m, 1:9], ALU.mult)
                        link(pool.tensor_tensor(w[r, T:T + 8], w[r, T:T + 8], p_inv[r, m, 9:17], ALU.mult))
                    for j, w in enumerate((wa, wb)):
                        r = slice(64 * j, 64 * j + 64)
                        ins = pool.tensor_tensor(up[r, 8:T + 8], w[r, 8:T + 8], up[r, 8:T + 8], ALU.subtract)
                    ins.then_inc(u_win, 1)
                elif kind == "uT":
                    s, m = step[1], step[2]
                    for j in range(2):
                        wait_released(pool, step, j)
                    pool.dma_start(mix_dram[s * TPS:(s + 1) * TPS, :, 6 + m, :].rearrange("c p t -> p c t"),
                                   wa[:, 0:T].rearrange("p (c t) -> p c t", c=TPS)).then_inc(po_st[s], 16)
                elif kind == "convT" and step[2] == 3:
                    s = step[1]
                    pool.wait_ge(dt_v, 4 * (s + 1))
                    for m in range(4):
                        wait_released(pool, ("convT", s, m))
                    decayed(pool, s, 1, TPS - 1, per_head, heads)
                elif kind == "sback" and step[2] > 1:
                    decayed(pool, step[1], 1, step[2] - 1, per_head, heads)
                elif kind == "sdec":
                    s, c = step[1], step[2]
                    k = nth(*step)
                    pool.wait_ge(z_st[k], 16)
                    pool.wait_ge(z_st[s * TPS + TPS - 1], 16)
                    if k:
                        wait_full(pool, ("sy",) + chunks[k - 1], 0)
                        pool.wait_ge(y_done, k)
                    for dr in range(2):
                        ins = pool.tensor_tensor(heads(xdt[:, dr, :]), heads(xs[:, c, :]),
                                                 per_head(dts[:, c, dr * 8:dr * 8 + 8], SSD_P), ALU.mult)
                    ins.then_inc(xdt_done, 1)
                    pool.dma_start(zg[:, :], z_dram[k]).then_inc(z_ld, 16)
                    if c < TPS - 1:
                        decayed(pool, s, 0, c, per_head, heads)
                elif kind == "sy":
                    k = nth(*step)
                    pool.wait_ge(ysq_done, k + 1)
                    if k:
                        pool.wait_ge(yn_done, k)
                    rsqrt(yrs[:, :], yms[:, :], yss[:, :], 1.0 / 256, 4 * EPS).then_inc(yrs_done, 1)
                elif kind == "sout":
                    s, c = step[1], step[2]
                    wait_released(pool, step)
                    pool.dma_start(mix_dram[s * TPS + c, :, 0:4, :], y1[:, :].rearrange("p (a b) -> p a b", a=4)).then_inc(ssd_st[s], 16)
                elif kind == "nav" and step[2] == 3:
                    s = step[1]
                    wait_released(pool, step)
                    for pair in range(2):
                        pool.dma_start(mix_dram[s * TPS:(s + 1) * TPS, :, 4 + pair, :].rearrange("c p t -> p c t"),
                                       nao[:, pair, :].rearrange("p (c t) -> p c t", c=TPS)).then_inc(nao_st[s], 16)

            wait_released(pool, ("router", NT - 1))
            pool.wait_ge(hn_st, 16 * NT)
            pool.iota(iota_e[:, :], [[1, NB + 1]], base=0, channel_multiplier=0, allow_small_or_imprecise_dtypes=True)
            pool.iota(iota_p[:, :], [[1, P]], base=0, channel_multiplier=0, allow_small_or_imprecise_dtypes=True)\
                .then_inc(r_pool, 1)
            pool.iota(token0[:, :], [[P, NT]], base=0, channel_multiplier=1, allow_small_or_imprecise_dtypes=True)\
                .then_inc(r_pool, 1)
            pool.iota(token1[:, :], [[P, NT]], base=1, channel_multiplier=1, allow_small_or_imprecise_dtypes=True)\
                .then_inc(r_pool, 1)
            pool.memset(xg[0][:, :], 0.0).then_inc(r_pool, 1)
            pool.memset(xg[1][:, :], 0.0).then_inc(r_pool, 1)
            pool.wait_ge(r_pool, 5)
            for j, ((h, lo), piece) in enumerate(zip(ew_parts(0), eraw)):
                pool.wait_ge(ew_high, j + 1)
                pool.tensor_tensor(lo, as_piece(piece, j), h.bitcast(F32), ALU.subtract).then_inc(ew_low, 1)
            pool.wait_ge(r_v, R_STAGES)

            last_token = pool.to_reg(NT * P - 1)

            def gather(n, i):
                pool.wait_ge(idc_done, n + 1)
                if not isinstance(n, int) or n > 1:
                    pool.wait_ge(xg_full, 2 * n - 2)
                if not isinstance(n, int) or n > 0:
                    pool.wait_ge(anchored, n)
                pool.tensor_tensor(anchor[:, :], token0[:, 0:1], token1[:, 0:1], ALU.add).then_inc(anchored, 1)
                pool.indirect_dma_start(out=xg[i][:, :], out_offset=None, in_=hn_dram,
                                        in_offset=bass.IndirectOffsetOnAxis(ap=idc[i][:, 0:1], axis=0),
                                        bounds_check=last_token, oob_is_err=False).then_inc(xg_ld[i], 16)

            def store(n, i, rows_=None):
                if rows_ is None:
                    rows_ = y_dram[n * P:(n + 1) * P, :] if isinstance(n, int) else y_dram[bass.ds(n * P, P), :]
                pool.wait_ge(y_lo, n + 1)
                pool.wait_ge(y_hi, n + 1)
                pool.dma_start(rows_, ey[i][:, :]).then_inc(ey_st[i], 16)

            gather(0, 0)
            gather(1, 1)
            gather(2, 0)

            def step(n, i, it):
                if not (isinstance(n, int) and n >= NE - 2):
                    gather(n + 2, i)
                store(n - 1, 1 - i)

            pipeline(pool, step)
            store(NE - 1, 1)
            pool.wait_ge(ey_st[0], 16 * (NE // 2))
            pool.wait_ge(ey_st[1], 16 * (NE // 2))

            pool.wait_ge(r_v, R_STAGES + 1)
            further_count = pool.value_load(ovi[0:1, NO:NO + 1], min_val=0, max_val=NO)
            with pool.If(further_count > 0):
                pool.dma_start(yo_dram.rearrange("(b p) d -> p b d", p=P),
                               ey[0][:, :].unsqueeze(1).to_broadcast([P, NO, D])).then_inc(fill_st, 16)
                pool.wait_ge(fill_st, 16)

            def more(b):
                n = b + NE
                gather(n, 0)
                store(n, 0, yo_dram[bass.ds(b * P, P), :])
                pool.wait_ge(ey_st[0], b * 16 + 16 * (NE // 2 + 1))

            further(pool, more)

            pool.wait_ge(ew_low, PIECES * NE)

            def fetch(i, c, also_further):
                if i >= 2:
                    pool.wait_ge(yg_used, 2 * (i - 2) + c + 1)
                if also_further:
                    pool.indirect_dma_start(out=yg[i % 2][c][:, :], out_offset=None, in_=yo_dram,
                                            in_offset=bass.IndirectOffsetOnAxis(ap=slot_o[:, c, i:i + 1], axis=0),
                                            bounds_check=NO * P - 1, oob_is_err=False).then_inc(yo_ld, 16)
                    pool.wait_ge(yo_ld, 16 * (2 * i + c + 1))
                pool.indirect_dma_start(out=yg[i % 2][c][:, :], out_offset=None, in_=y_dram,
                                        in_offset=bass.IndirectOffsetOnAxis(ap=slot[:, c, i:i + 1], axis=0),
                                        bounds_check=NE * P - 1, oob_is_err=False)\
                    .then_inc(yg_ld[i % 2][c], 16)

            for also_further in (False, True):
                with pool.If(further_count > 0 if also_further else further_count < 1):
                    for i in range(NT):
                        for c in range(2):
                            fetch(i, c, also_further)


def constants():
    tri = np.triu(np.ones((P, P), np.float32))
    inv = np.zeros((P, 2, 17), np.float32)
    for m in range(2):
        for j in range(2):
            w = 2 << (2 * m + j)
            t = np.concatenate([np.arange(8), np.arange(T - 8, T)])
            count = np.minimum(t + w // 2, T) - np.maximum(t - w // 2, 0)
            inv[64 * j:64 * j + 64, m, 0] = 1.0 / w
            inv[64 * j:64 * j + 64, m, 1:] = 1.0 / count
    key, qc = np.arange(2 * NA_KW)[None, :], (np.arange(P) % NA_KW)[:, None]
    mask = np.where((key >= qc) & (key < qc + NA_KW), 0.0, NEG).astype(np.float32)
    return {"c_mask": mask, "c_ident": np.eye(P, dtype=np.float32), "c_tri": np.stack([tri, tri.T]), "c_inv": inv}


def layouts(inputs):
    by_p = lambda a: a.reshape(-1, P).T
    twice = lambda a: np.concatenate([a, a])[:, None]
    i = {k: np.asarray(v)[0] for k, v in inputs.items() if k[:2] != "x_" and k[:3] != "mem"}
    conv = i["conv_w"].reshape(CONV_W, 6, P).transpose(2, 1, 0).reshape(P, 24)
    cols = [conv, by_p(i["conv_b"]), by_p(i["pool_scale"]), by_p(i["ssd_norm"]), twice(i["na_q_norm"]),
            twice(i["na_k_norm"]), i["xq_norm"][:, None], i["xk_norm"][:, None]]
    p, r = np.arange(P)[:, None, None], np.arange(ROWS)[None, :, None]
    j = np.arange(2 * NA_KW)[None, None, :]
    heads = i["na_rpb"].reshape(2, 2, RPB_R, RPB_C).transpose(1, 0, 2, 3)
    inner = heads[:, :, r - p // NA_KW + ROWS - 1, np.clip(j - p % NA_KW + 7, 0, RPB_C - 1)]
    j, side = j[:, :, :NA_KW], p // 64
    edge = heads[:, :, r - p % 64 // 8 + ROWS - 1, j - p % 8 + 15 - 8 * side]
    rows = [i["dt_bias"].ravel(), i["a_log"].ravel(), i["d_skip"]]
    return {"l_bias_in": np.ascontiguousarray(inner.transpose(2, 0, 1, 3, 4)),
            "l_bias_ed": np.ascontiguousarray(edge.transpose(2, 0, 1, 3, 4)), "l_cols": np.ascontiguousarray(np.concatenate(cols, 1)), "l_rows": np.concatenate(rows)}


_INS = ["x_prompt", "x_sample", "mem_prompt", "mem_sample", "norm_mix", "w_in", "conv_w", "conv_b", "dt_bias", "a_log",
        "d_skip", "ssd_norm", "na_q_norm", "na_k_norm", "na_rpb", "pool_w", "pool_scale", "w_out", "norm_xa",
        "norm_mem", "w_xq", "w_xkv", "xq_norm", "xk_norm", "w_xo", "norm_ffn", "w_router_group", "b_router_group",
        "w_router_expert", "b_router_expert", "w_e_gate", "w_e_up", "w_e_down"]


def kernel(**inputs):
    import concourse.bacc as _bacc
    from concourse.bass_utils import run_bass_kernel_spmd as _run

    nc = _bacc.Bacc("TRN2", target_bir_lowering=False, num_devices=1)
    arrays, dram = {}, {}
    for name in _INS:
        arrays[name] = np.ascontiguousarray(inputs[name])
    arrays.update(constants())
    arrays.update(layouts(inputs))
    for name, a in arrays.items():
        dram[name] = nc.dram_tensor(name, a.shape, mybir.dt.from_np(a.dtype), kind="ExternalInput").ap()
    outs = [nc.dram_tensor(n, (1, T, D), F32, kind="ExternalOutput").ap() for n in ("y_prompt", "y_sample")]
    dram["x"] = [dram["x_prompt"], dram["x_sample"]]
    dram["mem"] = [dram["mem_prompt"], dram["mem_sample"]]
    encoder_layer(nc, dram, outs)
    r = _run(nc, [arrays], core_ids=[0])
    return r.results[0]["y_prompt"], r.results[0]["y_sample"]
```
